# Optimizing a Trainium2 kernel written in Bass

```python
import math
import jax, jax.numpy as jnp
from jax import lax
import numpy as np

D_MODEL = 1024
BATCH = 1
SEQ = 512
DEPTH = 1

CONV_CH = D_MODEL
CONV_K = 3
N_HEADS = 8
HEAD_DIM = D_MODEL // (2 * N_HEADS)
V_DIM = 2 * HEAD_DIM
QK_WIDTH = N_HEADS * 2 * HEAD_DIM
ATTN_WIDTH = N_HEADS * V_DIM
ROPE_THETA = 10000.0
Q_BLOCK = 128
SPLIT_SIZES = (CONV_CH, CONV_CH, CONV_CH, QK_WIDTH, QK_WIDTH, ATTN_WIDTH, D_MODEL, D_MODEL)
IN_WIDTH = sum(SPLIT_SIZES)
SPLIT_POINTS = tuple(int(p) for p in np.cumsum(SPLIT_SIZES)[:-1])
PEER_HEADS = 8
PEER_QDIM = 256
PEER_HALF = PEER_QDIM // 2
N_KEYS = 128
N_EXPERTS = N_KEYS * N_KEYS
PEER_TOPK = 16
TOK_BLOCK = 128
RMS_EPS = 1e-6
NEG_INF = -1e30

kernel_name = 'hybrid_shortconv_diffattn_peer'

def rms_norm(x, g):
    xf = x.astype(jnp.float32)
    y = xf * lax.rsqrt(jnp.mean(xf * xf, axis=-1, keepdims=True) + RMS_EPS)
    return (y * g.astype(jnp.float32)).astype(x.dtype)

def rotary(x, pos):
    d = x.shape[-1]
    inv = ROPE_THETA ** (-jnp.arange(0, d, 2, dtype=jnp.float32) / d)
    ang = pos.astype(jnp.float32)[:, None] * inv[None, :]
    cos = jnp.cos(ang)[None, :, None, :]
    sin = jnp.sin(ang)[None, :, None, :]
    xf = x.astype(jnp.float32)
    x1, x2 = xf[..., : d // 2], xf[..., d // 2:]
    return jnp.concatenate([x1 * cos - x2 * sin, x2 * cos + x1 * sin], axis=-1).astype(x.dtype)

def short_conv_mixer(b, c, u, conv_w, w_out):
    z_in = c * u
    z = lax.conv_general_dilated(
        z_in, conv_w[:, None, :].astype(z_in.dtype), window_strides=(1,),
        padding=[(CONV_K - 1, 0)], dimension_numbers=('NWC', 'WIO', 'NWC'),
        feature_group_count=z_in.shape[-1])
    return (b * z) @ w_out

def diff_attention(q, k, v, lam, subln_g, lam_init):
    B, S = q.shape[0], q.shape[1]
    qh = jnp.transpose(q, (0, 2, 3, 1, 4))
    kh = jnp.transpose(k, (0, 2, 3, 1, 4))
    vh = jnp.transpose(v, (0, 2, 1, 3))
    scale = HEAD_DIM ** -0.5
    kpos = jnp.arange(S)

    def block(i):
        qb = lax.dynamic_slice_in_dim(qh, i * Q_BLOCK, Q_BLOCK, axis=3)
        s = jnp.einsum('bhmqd,bhmkd->bhmqk', qb, kh).astype(jnp.float32) * scale
        qpos = i * Q_BLOCK + jnp.arange(Q_BLOCK)
        mask = kpos[None, :] <= qpos[:, None]
        p = jax.nn.softmax(jnp.where(mask, s, NEG_INF), axis=-1)
        a = p[:, :, 0] - lam * p[:, :, 1]
        return jnp.einsum('bhqk,bhkd->bhqd', a.astype(vh.dtype), vh)

    o = lax.map(block, jnp.arange(S // Q_BLOCK))
    o = jnp.transpose(o, (1, 0, 3, 2, 4)).reshape(B, S, N_HEADS, V_DIM)
    o = rms_norm(o, subln_g) * (1.0 - lam_init)
    return o.reshape(B, S, ATTN_WIDTH)

def peer_ffn(xn, w_q, keys1, keys2, u_tab, v_tab):
    B, S, D = xn.shape
    q = (xn @ w_q).reshape(B, S, PEER_HEADS, 2, PEER_HALF)
    s1 = jnp.einsum('bshd,kd->bshk', q[..., 0, :], keys1).astype(jnp.float32)
    s2 = jnp.einsum('bshd,kd->bshk', q[..., 1, :], keys2).astype(jnp.float32)
    t1, i1 = lax.top_k(s1, PEER_TOPK)
    t2, i2 = lax.top_k(s2, PEER_TOPK)
    cand = (t1[..., :, None] + t2[..., None, :]).reshape(B, S, PEER_HEADS, PEER_TOPK * PEER_TOPK)
    top, ix = lax.top_k(cand, PEER_TOPK)
    e1 = jnp.take_along_axis(i1, ix // PEER_TOPK, axis=-1)
    e2 = jnp.take_along_axis(i2, ix % PEER_TOPK, axis=-1)
    experts = e1 * N_KEYS + e2
    gates = jax.nn.softmax(top, axis=-1).astype(xn.dtype)
    nb = S // TOK_BLOCK

    def to_blocks(a):
        return jnp.swapaxes(a.reshape((B, nb, TOK_BLOCK) + a.shape[2:]), 0, 1)

    def block(args):
        xb, eb, gb = args
        u = u_tab[eb]
        v = v_tab[eb]
        act = jax.nn.gelu(jnp.einsum('btd,bthkd->bthk', xb, u), approximate=False) * gb
        return jnp.einsum('bthk,bthkd->btd', act, v)

    y = lax.map(block, (to_blocks(xn), to_blocks(experts), to_blocks(gates)))
    return jnp.swapaxes(y, 0, 1).reshape(B, S, D)

def setup_inputs(seed: int = 0) -> dict:
    key = jax.random.key(seed)
    ks = jax.random.split(key, 20)
    f32 = jnp.float32
    nrm = lambda k, shape, s: jax.random.normal(k, shape, f32) * s
    return {
        'x': nrm(ks[0], (BATCH, SEQ, D_MODEL), 1.0),
        'norm1_g': 1.0 + nrm(ks[1], (DEPTH, D_MODEL), 0.02),
        'w_in': nrm(ks[2], (DEPTH, D_MODEL, IN_WIDTH), D_MODEL ** -0.5),
        'conv_w': nrm(ks[3], (DEPTH, CONV_K, CONV_CH), CONV_K ** -0.5),
        'w_out_conv': nrm(ks[4], (DEPTH, CONV_CH, D_MODEL), CONV_CH ** -0.5),
        'lambda_q1': nrm(ks[5], (DEPTH, HEAD_DIM), 0.1),
        'lambda_k1': nrm(ks[6], (DEPTH, HEAD_DIM), 0.1),
        'lambda_q2': nrm(ks[7], (DEPTH, HEAD_DIM), 0.1),
        'lambda_k2': nrm(ks[8], (DEPTH, HEAD_DIM), 0.1),
        'attn_subln_g': 1.0 + nrm(ks[9], (DEPTH, V_DIM), 0.02),
        'w_out_attn': nrm(ks[10], (DEPTH, ATTN_WIDTH, D_MODEL), ATTN_WIDTH ** -0.5),
        'w_o': nrm(ks[11], (DEPTH, D_MODEL, D_MODEL), D_MODEL ** -0.5),
        'norm2_g': 1.0 + nrm(ks[12], (DEPTH, D_MODEL), 0.02),
        'peer_w_q': nrm(ks[13], (DEPTH, D_MODEL, PEER_HEADS * PEER_QDIM), D_MODEL ** -0.5),
        'peer_keys1': nrm(ks[14], (DEPTH, N_KEYS, PEER_HALF), PEER_HALF ** -0.5),
        'peer_keys2': nrm(ks[15], (DEPTH, N_KEYS, PEER_HALF), PEER_HALF ** -0.5),
        'peer_u': nrm(ks[16], (DEPTH, N_EXPERTS, D_MODEL), D_MODEL ** -0.5),
        'peer_v': nrm(ks[17], (DEPTH, N_EXPERTS, D_MODEL), 0.1),
        'final_norm_g': 1.0 + nrm(ks[18], (D_MODEL,), 0.02),
    }

def reference(x, norm1_g, w_in, conv_w, w_out_conv, lambda_q1, lambda_k1, lambda_q2, lambda_k2,
              attn_subln_g, w_out_attn, w_o, norm2_g, peer_w_q, peer_keys1, peer_keys2,
              peer_u, peer_v, final_norm_g):
    B, S, _ = x.shape
    pos = jnp.arange(S, dtype=jnp.int32)
    h = x
    for l in range(DEPTH):
        lam_init = 0.8 - 0.6 * math.exp(-0.3 * l)
        xn = rms_norm(h, norm1_g[l])
        proj = xn @ w_in[l]
        cb, cc, cu, q, k, v, g_conv, g_attn = jnp.split(proj, SPLIT_POINTS, axis=-1)
        y_conv = short_conv_mixer(cb, cc, cu, conv_w[l], w_out_conv[l])
        q = rotary(q.reshape(B, S, 2 * N_HEADS, HEAD_DIM), pos).reshape(B, S, N_HEADS, 2, HEAD_DIM)
        k = rotary(k.reshape(B, S, 2 * N_HEADS, HEAD_DIM), pos).reshape(B, S, N_HEADS, 2, HEAD_DIM)
        lam = (jnp.exp(jnp.sum(lambda_q1[l].astype(jnp.float32) * lambda_k1[l].astype(jnp.float32)))
               - jnp.exp(jnp.sum(lambda_q2[l].astype(jnp.float32) * lambda_k2[l].astype(jnp.float32)))
               + lam_init)
        y_attn = diff_attention(q, k, v.reshape(B, S, N_HEADS, V_DIM), lam,
                                attn_subln_g[l], lam_init) @ w_out_attn[l]
        mixed = jax.nn.sigmoid(g_conv) * y_conv + jax.nn.sigmoid(g_attn) * y_attn
        h = h + mixed @ w_o[l]
        h = h + peer_ffn(rms_norm(h, norm2_g[l]), peer_w_q[l], peer_keys1[l], peer_keys2[l],
                         peer_u[l], peer_v[l])
    return rms_norm(h, final_norm_g)


_drawn_inputs = setup_inputs


def setup_inputs(seed=0):
    import zlib

    import numpy as np

    out = dict(_drawn_inputs(seed))
    spreads = {}
    factors = {'lambda_q1': 8.0,
     'lambda_k2': 3.805,
     'attn_subln_g': 6.305,
     'norm2_g': 8.0,
     'final_norm_g': 2.903}
    for name, (base, spread) in spreads.items():
        noise = np.random.default_rng([zlib.crc32(name.encode()), seed]).standard_normal(out[name].shape)
        drawn = base * np.exp(spread * noise) if base else spread * noise
        out[name] = __import__('jax').numpy.asarray(drawn.astype(out[name].dtype))
    for name, factor in factors.items():
        out[name] = (out[name] * factor).astype(out[name].dtype)
    return out
```

```python
from contextlib import ExitStack, contextmanager

import concourse.bass as bass
from concourse import mybir

F32 = mybir.dt.float32
F32R = mybir.dt.float32r
BF16 = mybir.dt.bfloat16
I32 = mybir.dt.int32
U32 = mybir.dt.uint32
ACT = mybir.ActivationFunctionType
ALU = mybir.AluOpType
AX = mybir.AxisListType

P = 128
D = 1024
T = 512
DC = D // P
TB = T // P
H = 8
HD = D // (2 * H)
KCONV = 3
PH = 8
TOPK = 16
NKEY = 128
LAM_INIT = 0.8 - 0.6
SCALE = HD ** -0.5
EPS = 1e-6
LOW = -3.0e38
RSQRT_MAGIC = 0x5F3759DF

L1_PRE = 3
L1_BODY = 6
N_L2 = L1_PRE + L1_BODY * H - 3
N_WO = N_L2 + 4 * DC
N_PQ = N_WO + DC
N_A = N_PQ + 2 * PH
N_B = N_A + NKEY
N_END = N_B + NKEY
SECTION = {"b": 0, "c": 1, "u": 2, "q": 3, "k": 4, "v": 5, "gc": 6, "ga": 7}
TOK = 16
BODIES = T // TOK


class Steps:

    def __init__(self, eng, sem):
        self.eng, self.sem, self.base, self.k, self.loops = eng, sem, 0, 0, []

    def value(self):
        v = self.base + self.k
        for i, per in self.loops:
            v = i * per + v
        return v

    def after(self, ins):
        self.end(ins)
        self.wait()

    def end(self, ins):
        ins.then_inc(self.sem, 1)
        self.k += 1

    def wait(self):
        self.eng.wait_ge(self.sem, self.value())

    @contextmanager
    def repeat(self, count, per):
        base, k = self.base, self.k
        with self.eng.Fori(0, count) as i:
            self.base, self.k = base + k, 0
            self.loops.append((i, per))
            yield i
            assert self.k == per, (self.k, per)
            self.loops.pop()
        self.base, self.k = base + k + count * per, 0


def peer_block(nc, x, norm_gains, w_in, conv_w, w_out_conv, lambdas, attn_subln_g, w_out_attn, w_o, peer_w_q,
               peer_keys, peer_u, peer_v, final_norm_g, c_cos, c_sin, c_ident, c_mask, c_iota, out):
    gel_dram = nc.dram_tensor("gelu_spill", (NKEY, P, T), F32, kind="Internal").ap()
    gate_dram = nc.dram_tensor("gate_spill", (BODIES, P, NKEY, TOK), F32, kind="Internal").ap()

    wo_v = w_o[0].rearrange("(c p) n -> c p n", p=P)
    v_v = peer_v[0].rearrange("(c p) d -> c p d", p=P)
    x_v = x[0].rearrange("(b p) d -> p b d", p=P)
    out_v = out[0].rearrange("(b p) d -> b p d", p=P)

    ctx = ExitStack()
    with ctx:
        def sem(name):
            return ctx.enter_context(nc.semaphore(name))

        def space(stack):
            return lambda name, shape, dt=F32: stack.enter_context(nc.sbuf_tensor(name, shape, dt))

        sb = space(ctx)
        ident = sb("ident", [P, P])
        iota_f = sb("iota_f", [P, P])
        iota_b = sb("iota_b", [P, P], BF16)
        zero_b = sb("zero_b", [P, T], BF16)
        norm_g = sb("norm_g", [P, 2, DC])
        gfin = sb("gfin", [P, D])
        xT_hi = sb("xT_hi", [P, DC, T], F32R)
        xT_lo = sb("xT_lo", [P, DC, T], F32R)
        w_raw = sb("w_raw", [P, 2, D])
        w_hi = sb("w_hi", [P, 2, D], F32R)
        w_lo = sb("w_lo", [P, 2, D], F32R)
        keysT_hi = sb("keysT_hi", [P, 2, NKEY], F32R)
        keysT_lo = sb("keysT_lo", [P, 2, NKEY], F32R)
        stat = sb("stat", [P, 4])
        rs_a = sb("rs_a", [P, 4])
        rs_i = sb("rs_i", [P, 4], I32)
        rs_t = sb("rs_t", [P, 4])
        rs_y = sb("rs_y", [P, 4])
        junk = sb("junk", [P, D])

        s0 = ExitStack()
        a = space(s0)
        x_sb = a("x_sb", [P, TB, D])
        keys_sb = a("keys_sb", [P, 2, NKEY])
        s0.close()
        sL = ExitStack()
        a = space(sL)
        attnT_hi = a("attnT_hi", [P, H, T], F32R)
        attnT_lo = a("attnT_lo", [P, H, T], F32R)
        bzT_hi = a("bzT_hi", [P, DC, T], F32R)
        bzT_lo = a("bzT_lo", [P, DC, T], F32R)
        s1 = ExitStack()
        a = space(s1)
        cos_t = a("cos_t", [P, T])
        sin_t = a("sin_t", [P, T])
        mask_t = a("mask_t", [P, P])
        cw = a("cw", [P, DC, KCONV])
        cw_h = a("cw_h", [P, KCONV])
        subln_g = a("subln_g", [P, 1])
        lam4 = a("lam4", [P, 4, HD])
        lam_p = a("lam_p", [P, 2, HD])
        lam_s = a("lam_s", [P, 2])
        neg_lam = a("neg_lam", [P, 1])
        qk_raw = a("qk_raw", [P, 2, T])
        qk_rot = a("qk_rot", [P, 2, T])
        rope_a = a("rope_a", [P, T])
        rope_b = a("rope_b", [P, T])
        qk_hi = a("qk_hi", [P, 2, T], F32R)
        qk_lo = a("qk_lo", [P, 2, T], F32R)
        vT_sb = a("vT_sb", [P, T])
        v_hi = a("v_hi", [P, TB, P], F32R)
        v_lo = a("v_lo", [P, TB, P], F32R)
        c_sb = a("c_sb", [P, T])
        u_sb = a("u_sb", [P, T])
        b_sb = a("b_sb", [P, T])
        cu = a("cu", [P, T + KCONV - 1])
        z_a = a("z_a", [P, T])
        z_b = a("z_b", [P, T])
        nbias = a("nbias", [P, 2, 2])
        nmax = a("nmax", [P, 2])
        prob = a("prob", [P, 2, 2, T])
        zsum = a("zsum", [P, 2, 2])
        rz = a("rz", [P, 2, 2])
        p1s = a("p1s", [P, T])
        dif = a("dif", [P, 2, T])
        difT_hi = a("difT_hi", [P, 2, TB, P], F32R)
        difT_lo = a("difT_lo", [P, 2, TB, P], F32R)
        on_sb = a("on_sb", [P, TB, P])
        s1.close()
        s2 = ExitStack()
        a = space(s2)
        mixT_hi = a("mixT_hi", [P, DC, T], F32R)
        mixT_lo = a("mixT_lo", [P, DC, T], F32R)
        sgc = a("sgc", [P, T])
        sga = a("sga", [P, T])
        yc_sb = a("yc_sb", [P, T])
        ya_sb = a("ya_sb", [P, T])
        m_a = a("m_a", [P, T])
        m_b = a("m_b", [P, T])
        m_c = a("m_c", [P, T])
        s2.close()
        sL.close()
        h_sb = sb("h_sb", [P, TB, D])
        sN = ExitStack()
        xn_2 = space(sN)("xn_2", [P, TB, D])
        sN.close()
        sP = ExitStack()
        a = space(sP)
        score = a("score", [P, TB, PH, 2, NKEY])
        q_hi = a("q_hi", [P, 2, T], F32R)
        q_lo = a("q_lo", [P, 2, T], F32R)
        gel = a("gel", [P, 2, T])
        sw = a("sw", [P, 2, NKEY])
        sw2 = a("sw2", [P, 2, NKEY])
        tval = a("tval", [P, 2, TOPK])
        tidx = a("tidx", [P, 2, TOPK], U32)
        tidx_b = a("tidx_b", [P, 2, TOPK], BF16)
        cand = a("cand", [P, TOPK, TOPK])
        cand2 = a("cand2", [P, TOPK * TOPK])
        cval = a("cval", [P, TOPK])
        cidx = a("cidx", [P, TOPK], U32)
        crank = a("crank", [P, 2, TOPK], U32)
        crank_b = a("crank_b", [P, 2 * TOPK, 2], BF16)
        pick = a("pick", [P, 2 * TOPK, TOPK], BF16)
        pick2 = a("pick2", [P, 2 * TOPK, TOPK], BF16)
        sel = a("sel", [P, 3, TB, PH, TOPK])
        gsum = a("gsum", [P, PH * TB])
        grec = a("grec", [P, PH * TB])
        selT = a("selT", [P, BODIES, 5, TOK])
        gpart = a("gpart", [P, T], BF16)
        grest = a("grest", [P, T])
        gateT = a("gateT", [P, T])
        tok5 = a("tok5", [P, 5 * TOK, 4], BF16)
        hit = a("hit", [P, 2, 8, NKEY], BF16)
        onehot = a("onehot", [P, 2, 4, 8, NKEY], BF16)
        g_stage = a("g_stage", [P, NKEY, TOK])
        sP.close()
        sB = ExitStack()
        a = space(sB)
        g_buf = a("g_buf", [P, 2, BODIES, 8, TOK])
        h_buf = a("h_buf", [P, 2, T])
        prod = a("prod", [P, 2, T])
        act_hi = a("act_hi", [P, 2, T], F32R)
        act_lo = a("act_lo", [P, 2, T], F32R)
        o_sb = a("o_sb", [P, TB, D])
        sB.close()

        bank = ctx.enter_context(nc.psum_tensor("bank", [P, 8, 512], F32))

        const_in = sem("const_in")
        x_in = sem("x_in")
        key_in = sem("key_in")
        consts_out = sem("consts_out")
        key_hi = sem("key_hi")
        key_lo = sem("key_lo")
        lam_exp = sem("lam_exp")
        lam_dot = sem("lam_dot")
        w_in_sem = [sem("w_landed0"), sem("w_landed1")]
        w_hi_done = sem("w_hi_done")
        w_lo_done = sem("w_lo_done")
        w_used = sem("w_used")
        bank_free = sem("bank_free")
        dve_own = sem("dve_own")
        n_sq = [sem(f"n{k}_squares") for k in (1, 2)]
        n_x = [sem(f"n{k}_scaled") for k in (1, 2)]
        n_t = [sem(f"n{k}_transposed") for k in (1, 2)]
        n_hi = [sem(f"n{k}_hi") for k in (1, 2)]
        n_lo = [sem(f"n{k}_lo") for k in (1, 2)]
        qk_ready = sem("qk_ready")
        cu_ready = sem("cu_ready")
        bz_ready = sem("bz_ready")
        scores_done = sem("scores_done")
        bias_ready = sem("bias_ready")
        exp_done = sem("exp_done")
        dif_ready = sem("dif_ready")
        t_full = sem("t_full")
        t_hi = sem("t_hi")
        t_lo = sem("t_lo")
        pv_done = sem("pv_done")
        o_squares = sem("o_squares")
        o_scale = sem("o_scale")
        on_ready = sem("on_ready")
        mix_done = sem("mix_done")
        h_ready = sem("h_ready")
        q_hi_done = sem("q_hi_done")
        q_done = sem("q_done")
        s_done = sem("s_done")
        s_copied = sem("s_copied")
        gel_done = sem("gel_done")
        gel_out = [sem("gel_stored0"), sem("gel_stored1")]
        top_shift = sem("top_shift")
        gate_exp = sem("gate_exp")
        sel_ready = sem("sel_ready")
        sel_used = sem("sel_used")
        selT_done = sem("selT_done")
        onehot_done = sem("onehot_done")
        g_full = sem("g_full")
        g_copied = sem("g_copied")
        g_out = sem("g_stored")
        gb_in = [sem("gates_landed0"), sem("gates_landed1")]
        hb_in = [sem("gelu_landed0"), sem("gelu_landed1")]
        prod_done = sem("prod_done")
        act_hi_done = sem("act_hi_done")
        act_lo_done = sem("act_lo_done")
        y_done = sem("y_done")
        y_sum = sem("y_sum")
        y_sq = sem("y_squares")
        o_ready = sem("o_ready")
        stored = sem("stored")

        block = ctx.enter_context(nc.Block())

        def w_tile(t, n):
            return t[:, n % 2, :].rearrange("p (c n) -> p c n", c=DC)

        @block.sync
        def _(sp):
            sp.dma_start(x_sb[:], x_v).then_inc(x_in, 16)
            sp.dma_start(ident[:], c_ident).then_inc(const_in, 16)
            sp.dma_start(iota_f[:], c_iota).then_inc(const_in, 16)
            sp.dma_start(norm_g[:], norm_gains).then_inc(const_in, 16)
            sp.dma_start(gfin[:], final_norm_g.partition_broadcast(P)).then_inc(const_in, 16)
            sp.dma_start(keys_sb[:], peer_keys).then_inc(key_in, 16)

            def load(n, par, src):
                sp.wait_ge(w_lo_done, n + 1)
                s = par % 2
                sp.dma_start(w_raw[:, s, :], src).then_inc(w_in_sem[s], 16)

            def section(name, h):
                return w_in[bass.ds(h + SECTION[name] * DC, 1)]

            for n, name in enumerate("qkv"):
                load(n, n, section(name, 0))
            sp.dma_start(cos_t[:], c_cos).then_inc(consts_out, 16)
            sp.dma_start(sin_t[:], c_sin).then_inc(consts_out, 16)
            sp.dma_start(mask_t[:], c_mask).then_inc(consts_out, 16)
            sp.dma_start(cw[:], conv_w).then_inc(consts_out, 16)
            sp.dma_start(subln_g[:], attn_subln_g[0].rearrange("(p a) -> p a", a=1)).then_inc(consts_out, 16)
            sp.dma_start(lam4[:], lambdas.partition_broadcast(P)).then_inc(consts_out, 16)
            with sp.Fori(0, H - 1) as h:
                for j, name in enumerate("cub"):
                    load(h * L1_BODY + (L1_PRE + j), L1_PRE + j, section(name, h))
                for j, name in enumerate("qkv"):
                    load(h * L1_BODY + (L1_PRE + 3 + j), L1_PRE + 3 + j, section(name, h + 1))
            for j, name in enumerate("cub"):
                load((H - 1) * L1_BODY + L1_PRE + j, L1_PRE + j, section(name, H - 1))
            with sp.Fori(0, DC) as i:
                load(i * 4 + N_L2, 0, section("gc", i))
                load(i * 4 + (N_L2 + 1), 1, section("ga", i))
                load(i * 4 + (N_L2 + 2), 0, w_out_conv[bass.ds(i, 1)])
                load(i * 4 + (N_L2 + 3), 1, w_out_attn[bass.ds(i, 1)])
            for c in range(DC):
                load(N_WO + c, N_WO + c, wo_v[c])
                if c == 1:
                    sp.wait_ge(w_used, N_WO + 2)
                    sp.dma_start(h_sb[:], x_v).then_inc(x_in, 16)
            with sp.Fori(0, PH) as h:
                for c in range(2):
                    load(h * 2 + (N_PQ + c), N_PQ + c, peer_w_q[bass.ds(h * 2 + c, 1)])

            for c in range(2):
                load(N_A + c, N_A + c, peer_u[c])

            def a_chunk(c, k, src):
                load(c + (N_A + 2), k, src)
                sp.wait_ge(gel_done, c + 3)
                sp.dma_start(gel_dram[bass.ds(c, 1)], gel[:, k]).then_inc(gel_out[k], 16)

            def a2_store(i):
                sp.wait_ge(g_copied, i * 4 + 6)
                sp.dma_start(gate_dram[bass.ds(i, 1)], g_stage[:]).then_inc(g_out, 16)

            with sp.Fori(0, 32) as i:
                for k in range(2):
                    a_chunk(i * 2 + k, k, peer_u[bass.ds(i * 2 + (2 + k), 1)])
            with sp.Fori(0, 31) as i:
                for k in range(2):
                    a_chunk(i * 2 + (64 + k), k, peer_u[bass.ds(i * 2 + (66 + k), 1)])
                a2_store(i)
            for k in range(2):
                a_chunk(126 + k, k, v_v[k])
            a2_store(31)

            for k in range(2):
                sp.wait_ge(gel_out[k], 16 * 65)
            sp.wait_ge(g_out, 16 * (BODIES + 1))
            sp.wait_ge(g_full, T // 4 + 3)

            def gates(block_of_8, s):
                src = gate_dram[:, :, bass.ds(block_of_8 * 8, 8), :].rearrange("b p e t -> p b e t")
                for q in range(2):
                    sp.dma_start(g_buf[:, s, q * (BODIES // 2):(q + 1) * (BODIES // 2)],
                                 src[:, q * (BODIES // 2):(q + 1) * (BODIES // 2)]).then_inc(gb_in[s], 16)

            def gelus(c, k):
                sp.dma_start(h_buf[:, k], gel_dram[bass.ds(c, 1)]).then_inc(hb_in[k], 16)

            for s in range(2):
                gates(s, s)
            for k in range(2):
                gelus(k, k)

            def b_chunks(c, last=False):
                for k in range(2):
                    load(c + (N_B + 2 + k), k, v_v[bass.ds(c + (2 + k), 1)])
                    sp.wait_ge(prod_done, c + (3 + k))
                    gelus(c + (2 + k), k)

            with sp.Fori(0, 7) as o:
                for s in range(2):
                    with sp.Fori(0, 4) as r:
                        b_chunks(o * 16 + r * 2 + 8 * s)
                    sp.wait_ge(prod_done, o * 16 + (8 * s + 10))
                    gates(o * 2 + (2 + s), s)
            with sp.Fori(0, 7) as r:
                b_chunks(r * 2 + 112)
            for b in range(TB):
                sp.wait_ge(o_ready, b + 1)
                sp.dma_start(out_v[b], o_sb[:, b]).then_inc(stored, 16)
            sp.wait_ge(stored, 16 * TB)

        @block.gpsimd
        def _(pool):
            for s, n in ((w_lo_done, 2), (w_used, 2), (bank_free, 2), (cu_ready, 1), (bz_ready, 1),
                         (exp_done, 2), (dif_ready, 2), (t_lo, 1), (pv_done, 2), (on_ready, 1), (o_squares, 1), (qk_ready, 1),
                         (mix_done, 1), (q_done, 2), (s_done, 2), (s_copied, 2), (gel_done, 2), (gel_out[0], 16), (gel_out[1], 16),
                         (g_full, 3), (g_copied, 2), (g_out, 16), (prod_done, 2), (act_lo_done, 2), (onehot_done, 1)):
                pool.sem_inc(s, n)

        @block.scalar
        def _(act):
            def copy(dst, src, **kw):
                return act.activation(dst, src, ACT.Copy, **kw)

            def split_hi(n, par):
                s = par % 2
                act.wait_ge(w_in_sem[s], (n - s) * 8 + 16)
                act.wait_ge(w_used, n + 1)
                copy(w_hi[:, s, :], w_raw[:, s, :]).then_inc(w_hi_done, 1)

            def norm(k, src, ready):
                for b in range(TB):
                    ready(b)
                    if b:
                        act.wait_ge(n_sq[k], b)
                    act.activation(junk[:], src[:, b], ACT.Square, accum_out=stat[:, b:b + 1]).then_inc(n_sq[k], 1)
                if k == 0:
                    act.wait_ge(key_in, 16)
                    copy(keysT_hi[:], keys_sb[:]).then_inc(key_hi, 1)
                for c in range(DC):
                    act.wait_ge(n_t[k], c + 1)
                    copy(xT_hi[:, c], bank[:, c], scale=norm_g[:, k, c:c + 1]).then_inc(n_hi[k], 1)

            act.wait_ge(x_in, 16)
            act.wait_ge(const_in, 16 * 4)
            norm(0, x_sb, lambda b: None)
            split_hi(0, 0)
            split_hi(1, 1)
            act.wait_ge(lam_dot, 2)
            act.activation(lam_s[:], lam_s[:], ACT.Exp).then_inc(lam_exp, 1)

            def evac(n, par):
                act.wait_ge(w_used, n + 3)
                return bank[:, par % 2]

            def out_qk(n, par, which, h, first=False):
                src = evac(n, par)
                if not first:
                    act.wait_ge(qk_ready, h * 2 + which)
                copy(qk_raw[:, which], src)
                for q in range(4):
                    d = q ^ 1
                    last = copy(qk_rot[32 * d:32 * d + 32, which], src[32 * q:32 * q + 32])
                last.then_inc(bank_free, 1)

            def t_out(v, dst, scale=None):
                act.wait_ge(t_full, v + 1)
                n = dst.shape[1]
                src = bank[:, 6, 0:n * P].rearrange("p (c n) -> p c n", c=n)
                kw = {} if scale is None else {"scale": scale}
                copy(dst, src, **kw).then_inc(t_hi, 1)

            def exps(U, u):
                sp_, nk = u % 2, (u + 1) * P
                act.wait_ge(bias_ready, U + 1)
                act.wait_ge(dif_ready, U + 1)
                for m in range(2):
                    ins = act.activation(prob[:, sp_, m, 0:nk], bank[:, 2 + 2 * sp_ + m, 0:nk], ACT.Exp,
                                         bias=nbias[:, sp_, m:m + 1], scale=SCALE,
                                         accum_out=zsum[:, sp_, m:m + 1])
                ins.then_inc(exp_done, 1)

            def squares(U, u):
                act.wait_ge(o_squares, U + 1)
                act.activation(junk[:, 0:P], bank[:, 7, u * P:(u + 1) * P], ACT.Square,
                               accum_out=stat[:, u:u + 1]).then_inc(o_squares, 1)

            def l1_body(h, last):
                n = h * L1_BODY + L1_PRE
                U = h * 4
                V = h * 6
                act.wait_ge(cu_ready, h + 1)
                copy(c_sb[:], evac(n, 1)).then_inc(bank_free, 1)
                split_hi(n + 2, 1)
                t_out(V, v_hi[:])
                exps(U, 0)
                exps(U + 1, 1)
                copy(u_sb[:], evac(n + 1, 0)).then_inc(bank_free, 1)
                split_hi(n + 3, 0)
                act.wait_ge(pv_done, U + 1)
                t_out(V + 1, difT_hi[:, 0, 0:1])
                exps(U + 2, 2)
                act.wait_ge(pv_done, U + 2)
                t_out(V + 2, difT_hi[:, 1, 0:2])
                exps(U + 3, 3)
                act.wait_ge(bz_ready, h + 1)
                copy(b_sb[:], evac(n + 2, 1)).then_inc(bank_free, 1)
                split_hi(n + 4, 1)
                t_out(V + 3, difT_hi[:, 0, 0:3])
                t_out(V + 4, difT_hi[:, 1, 0:4])
                if not last:
                    out_qk(n + 3, 0, 0, h + 1)
                    split_hi(n + 5, 0)
                act.wait_ge(pv_done, U + TB + 2)
                for u in range(TB):
                    squares(U + u, u)
                act.wait_ge(o_scale, h + 1)
                for u in range(TB):
                    ins = copy(on_sb[:, u], bank[:, 7, u * P:(u + 1) * P], scale=rs_y[:, u:u + 1])
                ins.then_inc(on_ready, 1)
                if not last:
                    out_qk(n + 4, 1, 1, h + 1)
                    split_hi(n + 6, 1)
                act.wait_ge(t_full, V + 6)
                copy(attnT_hi[:, bass.ds(h, 1)], bank[:, 6].unsqueeze(1), scale=subln_g[:, 0:1]).then_inc(t_hi, 1)
                if not last:
                    copy(vT_sb[:], evac(n + 5, 0)).then_inc(bank_free, 1)
                    split_hi(n + 7, 0)

            act.wait_ge(consts_out, 16 * 6)
            out_qk(0, 0, 0, 0, first=True)
            split_hi(2, 0)
            out_qk(1, 1, 1, 0, first=True)
            split_hi(3, 1)
            copy(vT_sb[:], evac(2, 0)).then_inc(bank_free, 1)
            split_hi(4, 0)
            with act.Fori(0, H - 1) as h:
                l1_body(h, False)
            l1_body(H - 1, True)

            act.wait_ge(t_lo, 6 * H + 1)
            with act.Fori(0, DC) as i:
                n = i * 4 + N_L2
                act.wait_ge(mix_done, i + 1)
                act.activation(sgc[:], evac(n, 0), ACT.Sigmoid).then_inc(bank_free, 1)
                split_hi(n + 2, 0)
                act.activation(sga[:], evac(n + 1, 1), ACT.Sigmoid).then_inc(bank_free, 1)
                split_hi(n + 3, 1)
                copy(yc_sb[:], evac(n + 2, 0)).then_inc(bank_free, 1)
                split_hi(n + 4, 0)
                copy(ya_sb[:], evac(n + 3, 1)).then_inc(bank_free, 1)
                split_hi(n + 5, 1)
            for c in range(DC):
                split_hi(N_WO + c + 2, c)
            norm(1, h_sb, lambda b: act.wait_ge(h_ready, 2 * b + 2))

            def q_out(s, c):
                act.wait_ge(w_used, s + (N_PQ + 3))
                act.wait_ge(s_done, s + 1)
                copy(q_hi[:, c], bank[:, c]).then_inc(q_hi_done, 1)

            def s_out(h, s, c):
                act.wait_ge(s_done, s + 3)
                copy(score[:, :, bass.ds(h, 1), c],
                     bank[:, 2 + c].rearrange("p (b a n) -> p b a n", a=1, b=TB)).then_inc(s_copied, 1)

            q_out(0, 0)
            split_hi(N_PQ + 2, 0)
            with act.Fori(0, PH - 1) as h:
                s = h * 2
                q_out(s + 1, 1)
                split_hi(s + (N_PQ + 3), 1)
                s_out(h, s, 0)
                q_out(s + 2, 0)
                split_hi(s + (N_PQ + 4), 0)
                s_out(h, s + 1, 1)
            q_out(15, 1)
            split_hi(N_PQ + 17, 1)
            s_out(PH - 1, 14, 0)
            s_out(PH - 1, 15, 1)

            def gelu(c, k, split=True):
                act.wait_ge(w_used, c + (N_A + 3))
                act.wait_ge(gel_out[k], (c - k) * 8 + 16)
                act.activation(gel[:, k], bank[:, 4 + k], ACT.Gelu).then_inc(gel_done, 1)
                if split:
                    split_hi(c + (N_A + 2), k)

            def g_group(g, slot, k):
                act.wait_ge(g_full, g + 4)
                copy(g_stage[:, :, 4 * k:4 * k + 4], bank[:, 6 + slot].rearrange("p (t e) -> p e t", t=4))\
                    .then_inc(g_copied, 1)

            with act.Fori(0, 32) as i:
                gelu(i * 2, 0)
                gelu(i * 2 + 1, 1)
            act.wait_ge(top_shift, 1)
            act.activation(sel[:, 2], sel[:, 2], ACT.Exp).then_inc(gate_exp, 1)

            def a2_body(i, last):
                c = i * 2 + 64
                gelu(c, 0)
                act.wait_ge(g_out, i * 16 + 16)
                g_group(i * 4, 0, 0)
                g_group(i * 4 + 1, 1, 1)
                gelu(c + 1, 1, split=not last)
                g_group(i * 4 + 2, 0, 2)
                g_group(i * 4 + 3, 1, 3)

            with act.Fori(0, 31) as i:
                a2_body(i, False)
            a2_body(31, True)

            def b_chunk(c, k, split=True):
                act.wait_ge(prod_done, c + 3)
                act.wait_ge(w_used, c + (N_B + 1))
                copy(act_hi[:, k], prod[:, k]).then_inc(act_hi_done, 1)
                if split:
                    split_hi(c + (N_B + 1), k + 1)

            with act.Fori(0, 63) as i:
                for k in range(2):
                    b_chunk(i * 2 + k, k)
            b_chunk(126, 0)
            b_chunk(127, 1, split=False)
            for b in range(TB):
                act.wait_ge(y_sum, 2 * b + 2)
                if b:
                    act.wait_ge(y_sq, b)
                act.activation(junk[:], h_sb[:, b], ACT.Square, accum_out=stat[:, b:b + 1]).then_inc(y_sq, 1)

        @block.vector
        def _(dve):
            v = nc.vector
            own = Steps(dve, dve_own)

            def split_lo(n, par):
                s = par % 2
                dve.wait_ge(w_hi_done, n + 1)
                v.tensor_tensor(w_lo[:, s, :], w_raw[:, s, :], w_hi[:, s, :].bitcast(F32), ALU.subtract)\
                    .then_inc(w_lo_done, 1)

            def rsqrt(width):
                own.after(v.tensor_scalar(rs_a[:], stat[:], 1.0 / width, EPS, ALU.mult, ALU.add))
                own.after(v.tensor_single_scalar(rs_i[:], rs_a[:].bitcast(I32), 1, ALU.arith_shift_right))
                own.after(v.tensor_scalar(rs_y[:].bitcast(I32), rs_i[:], -1.0, float(RSQRT_MAGIC), ALU.mult, ALU.add))
                for k in range(3):
                    own.after(v.tensor_tensor(rs_t[:], rs_y[:], rs_y[:], ALU.mult))
                    own.after(v.tensor_tensor(rs_t[:], rs_t[:], rs_a[:], ALU.mult))
                    own.after(v.tensor_scalar(rs_t[:], rs_t[:], -0.5, 1.5, ALU.mult, ALU.add))
                    ins = v.tensor_tensor(rs_y[:], rs_y[:], rs_t[:], ALU.mult)
                    if k < 2:
                        own.after(ins)
                return ins

            def norm(k, src, tile):
                dve.wait_ge(n_sq[k], TB)
                own.after(rsqrt(D))
                for b in range(TB):
                    v.tensor_scalar(tile[:, b], src[:, b], rs_y[:, b:b + 1], None, ALU.mult).then_inc(n_x[k], 1)
                for c in range(DC):
                    dve.wait_ge(n_hi[k], c + 1)
                    v.scalar_tensor_tensor(xT_lo[:, c], bank[:, c], norm_g[:, k, c:c + 1],
                                           xT_hi[:, c].bitcast(F32), ALU.mult, ALU.subtract).then_inc(n_lo[k], 1)

            v.memset(zero_b[:], 0.0)
            dve.wait_ge(const_in, 16 * 4)
            v.tensor_copy(iota_b[:], iota_f[:])
            dve.wait_ge(key_hi, 1)
            v.tensor_tensor(keysT_lo[:], keys_sb[:], keysT_hi[:].bitcast(F32), ALU.subtract).then_inc(key_lo, 1)
            norm(0, x_sb, x_sb)
            split_lo(0, 0)
            split_lo(1, 1)
            dve.wait_ge(consts_out, 16 * 6)
            own.after(v.tensor_tensor(lam_p[:, 0], lam4[:, 0], lam4[:, 1], ALU.mult))
            own.after(v.tensor_tensor(lam_p[:, 1], lam4[:, 2], lam4[:, 3], ALU.mult))
            for k in range(2):
                v.tensor_reduce(lam_s[:, k:k + 1], lam_p[:, k], AX.X, ALU.add).then_inc(lam_dot, 1)
            own.after(v.memset(cu[:, 0:KCONV - 1], 0.0))
            own.after(v.tensor_scalar(subln_g[:], subln_g[:], 1.0 - LAM_INIT, None, ALU.mult))
            dve.wait_ge(lam_exp, 1)
            own.after(v.tensor_tensor(neg_lam[:], lam_s[:, 1:2], lam_s[:, 0:1], ALU.subtract))
            own.after(v.tensor_scalar(neg_lam[:], neg_lam[:], -LAM_INIT, None, ALU.add))

            def rope(which, h):
                n = h * L1_BODY + which
                dve.wait_ge(bank_free, n + 3)
                dve.wait_ge(qk_ready, h * 2 + (which + 1))
                own.after(v.tensor_tensor(rope_a[:], qk_raw[:, which], cos_t[:], ALU.mult))
                own.after(v.tensor_tensor(rope_b[:], qk_rot[:, which], sin_t[:], ALU.mult))
                own.after(v.tensor_tensor(rope_a[:], rope_a[:], rope_b[:], ALU.add))
                own.after(v.tensor_copy(qk_hi[:, which], rope_a[:]))
                v.tensor_tensor(qk_lo[:, which], rope_a[:], qk_hi[:, which].bitcast(F32), ALU.subtract)\
                    .then_inc(qk_ready, 1)

            def t_out(V, hi, lo):
                dve.wait_ge(t_hi, V + 1)
                n = hi.shape[1]
                src = bank[:, 6, 0:n * P].rearrange("p (c n) -> p c n", c=n)
                v.tensor_tensor(lo, src, hi.bitcast(F32), ALU.subtract).then_inc(t_lo, 1)

            def mask_max(U, u):
                s, nk = u % 2, (u + 1) * P
                dve.wait_ge(scores_done, U + 1)
                diag = bank[:, 2 + 2 * s:4 + 2 * s, u * P:nk]
                own.after(v.tensor_tensor(diag, diag, mask_t[:].unsqueeze(1).to_broadcast([P, 2, P]), ALU.add))
                own.after(v.tensor_reduce(nmax[:], bank[:, 2 + 2 * s:4 + 2 * s, 0:nk], AX.X, ALU.max, negate=True))
                v.tensor_scalar(nbias[:, s], nmax[:], SCALE, None, ALU.mult).then_inc(bias_ready, 1)

            def combine(U, u):
                s, nk = u % 2, (u + 1) * P
                dve.wait_ge(exp_done, U + 3)
                own.after(v.reciprocal(rz[:, s], zsum[:, s]))
                own.after(v.tensor_scalar(p1s[:, 0:nk], prob[:, s, 1, 0:nk], rz[:, s, 1:2], neg_lam[:, 0:1],
                                          ALU.mult, ALU.mult))
                v.scalar_tensor_tensor(dif[:, s, 0:nk], prob[:, s, 0, 0:nk], rz[:, s, 0:1], p1s[:, 0:nk],
                                       ALU.mult, ALU.add).then_inc(dif_ready, 1)

            def l1_body(h, last):
                n = h * L1_BODY + L1_PRE
                U = h * 4
                V = h * 6
                split_lo(n + 2, 1)
                t_out(V, v_hi[:], v_lo[:])
                mask_max(U, 0)
                mask_max(U + 1, 1)
                combine(U, 0)
                combine(U + 1, 1)
                own.after(v.tensor_copy(cw_h[:].unsqueeze(1), cw[:, bass.ds(h, 1)]))
                split_lo(n + 3, 0)
                dve.wait_ge(bank_free, n + 4)
                v.tensor_tensor(cu[:, 2:2 + T], c_sb[:], u_sb[:], ALU.mult).then_inc(cu_ready, 1)
                t_out(V + 1, difT_hi[:, 0, 0:1], difT_lo[:, 0, 0:1])
                mask_max(U + 2, 2)
                t_out(V + 2, difT_hi[:, 1, 0:2], difT_lo[:, 1, 0:2])
                mask_max(U + 3, 3)
                combine(U + 2, 2)
                combine(U + 3, 3)
                own.after(v.tensor_scalar(z_a[:], cu[:, 0:T], cw_h[:, 0:1], None, ALU.mult))
                own.after(v.scalar_tensor_tensor(z_b[:], cu[:, 1:1 + T], cw_h[:, 1:2], z_a[:], ALU.mult, ALU.add))
                own.after(v.scalar_tensor_tensor(z_a[:], cu[:, 2:2 + T], cw_h[:, 2:3], z_b[:], ALU.mult, ALU.add))
                split_lo(n + 4, 1)
                dve.wait_ge(bank_free, n + 5)
                own.after(v.tensor_tensor(z_b[:], z_a[:], b_sb[:], ALU.mult))
                own.after(v.tensor_copy(bzT_hi[:, bass.ds(h, 1)], z_b[:].unsqueeze(1)))
                v.tensor_tensor(bzT_lo[:, bass.ds(h, 1)], z_b[:].unsqueeze(1),
                                bzT_hi[:, bass.ds(h, 1)].bitcast(F32), ALU.subtract).then_inc(bz_ready, 1)
                t_out(V + 3, difT_hi[:, 0, 0:3], difT_lo[:, 0, 0:3])
                t_out(V + 4, difT_hi[:, 1, 0:4], difT_lo[:, 1, 0:4])
                if not last:
                    split_lo(n + 5, 0)
                dve.wait_ge(o_squares, h * 4 + 5)
                rsqrt(P).then_inc(o_scale, 1)
                if not last:
                    rope(0, h + 1)
                    split_lo(n + 6, 1)
                    rope(1, h + 1)
                dve.wait_ge(t_hi, V + 6)
                v.scalar_tensor_tensor(attnT_lo[:, bass.ds(h, 1)], bank[:, 6].unsqueeze(1), subln_g[:, 0:1],
                                       attnT_hi[:, bass.ds(h, 1)].bitcast(F32), ALU.mult, ALU.subtract)\
                    .then_inc(t_lo, 1)
                if not last:
                    split_lo(n + 7, 0)

            split_lo(2, 0)
            rope(0, 0)
            split_lo(3, 1)
            rope(1, 0)
            split_lo(4, 0)
            with own.repeat(H - 1, 36 + 8) as h:
                l1_body(h, False)
            l1_body(H - 1, True)

            with own.repeat(DC, 4) as i:
                n = i * 4 + N_L2
                split_lo(n + 2, 0)
                split_lo(n + 3, 1)
                split_lo(n + 4, 0)
                dve.wait_ge(bank_free, n + 5)
                own.after(v.tensor_tensor(m_a[:], sgc[:], yc_sb[:], ALU.mult))
                split_lo(n + 5, 1)
                dve.wait_ge(bank_free, n + 6)
                own.after(v.tensor_tensor(m_b[:], sga[:], ya_sb[:], ALU.mult))
                own.after(v.tensor_tensor(m_c[:], m_a[:], m_b[:], ALU.add))
                own.after(v.tensor_copy(mixT_hi[:, bass.ds(i, 1)], m_c[:].unsqueeze(1)))
                v.tensor_tensor(mixT_lo[:, bass.ds(i, 1)], m_c[:].unsqueeze(1),
                                mixT_hi[:, bass.ds(i, 1)].bitcast(F32), ALU.subtract).then_inc(mix_done, 1)
            for c in range(DC):
                split_lo(N_WO + c + 2, c)
            dve.wait_ge(w_used, N_PQ + 2)
            dve.wait_ge(x_in, 32)
            for b in range(TB):
                for q in range(2):
                    half = h_sb[:, b, q * 512:(q + 1) * 512]
                    v.tensor_tensor(half, bank[:, 2 * b + q], half, ALU.add).then_inc(h_ready, 1)
            norm(1, h_sb, xn_2)

            def q_out(s, c):
                dve.wait_ge(q_hi_done, s + 1)
                v.tensor_tensor(q_lo[:, c], bank[:, c], q_hi[:, c].bitcast(F32), ALU.subtract).then_inc(q_done, 1)

            q_out(0, 0)
            split_lo(N_PQ + 2, 0)
            with dve.Fori(0, PH - 1) as h:
                s = h * 2
                q_out(s + 1, 1)
                split_lo(s + (N_PQ + 3), 1)
                q_out(s + 2, 0)
                split_lo(s + (N_PQ + 4), 0)
            q_out(15, 1)
            split_lo(N_PQ + 17, 1)

            units = score[:].rearrange("p b h c n -> p (b h) c n")
            cand_flat = cand[:].rearrange("p a b -> p (a b)")
            val_out = sel[:, 2].rearrange("p b h k -> p (b h) k")
            key_out = sel[:, 0:2].rearrange("p c b h k -> p c (b h) k")

            def unit_step(i, j, halves, pairs, between=None):
                jobs = []
                if pairs:
                    jobs.append((cval, cidx, cand_flat, cand2[:]))
                if halves:
                    jobs += [(tval[:, c], tidx[:, c], sw[:, c], sw2[:, c]) for c in range(2)]
                if pairs:
                    v.tensor_copy(tidx_b[:], tidx[:])
                    v.tensor_tensor(cand[:], tval[:, 0].unsqueeze(2).to_broadcast([P, TOPK, TOPK]),
                                    tval[:, 1].unsqueeze(1).to_broadcast([P, TOPK, TOPK]), ALU.add)
                if halves:
                    v.tensor_copy(sw[:].unsqueeze(1), units[:, bass.ds(j, 1)])
                dve.drain()
                for val, idx, src, spare in jobs:
                    v.max(val[:, 0:8], src)
                dve.drain()
                for val, idx, src, spare in jobs:
                    v.match_replace(spare, val[:, 0:8], src, LOW)
                    v.max_index(idx[:, 0:8], val[:, 0:8], src)
                dve.drain()
                for val, idx, src, spare in jobs:
                    v.max(val[:, 8:16], spare)
                dve.drain()
                for val, idx, src, spare in jobs:
                    v.max_index(idx[:, 8:16], val[:, 8:16], spare)
                if between:
                    between()
                dve.drain()
                if not pairs:
                    return
                v.tensor_copy(val_out[:, bass.ds(i, 1)], cval[:].unsqueeze(1))
                v.tensor_single_scalar(crank[:, 0], cidx[:], 4, ALU.arith_shift_right)
                v.tensor_single_scalar(crank[:, 1], cidx[:], TOPK - 1, ALU.bitwise_and)
                dve.drain()
                v.tensor_copy(crank_b[:], crank[:].rearrange("p c k -> p (c k)").unsqueeze(2).to_broadcast([P, 2 * TOPK, 2]))
                dve.drain()
                shape = [P, 2 * TOPK, TOPK // 2, 2]
                v.tensor_tensor(pick[:].rearrange("p r (k j) -> p r k j", j=2),
                                crank_b[:].unsqueeze(2).to_broadcast(shape),
                                iota_b[:, 0:TOPK].rearrange("p (k j) -> p k j", j=2).unsqueeze(1).to_broadcast(shape),
                                ALU.is_equal)
                dve.drain()
                by_half = [t[:].rearrange("p (c r) k -> p c r k", c=2) for t in (pick, pick2)]
                v.tensor_tensor(by_half[1], by_half[0],
                                tidx_b[:].unsqueeze(2).to_broadcast([P, 2, TOPK, TOPK]), ALU.mult)
                dve.drain()
                for c in range(2):
                    v.tensor_reduce(key_out[:, c, bass.ds(i, 1)], by_half[1][:, c].unsqueeze(1), AX.X, ALU.add)

            dve.wait_ge(s_copied, 2 * PH + 2)
            v.tensor_copy(sw[:].unsqueeze(1), units[:, 0:1])
            dve.drain()
            unit_step(0, 0, True, False)
            with dve.Fori(0, 31) as i:
                c = i * 2
                unit_step(i, i + 1, True, True, lambda: split_lo(c + (N_A + 2), 0))
                split_lo(c + (N_A + 3), 1)
            unit_step(31, 0, False, True, lambda: split_lo(N_A + 64, 0))
            split_lo(N_A + 65, 1)
            dve.drain()

            top = sel[:, 2].rearrange("p b h k -> p (b h) k")
            best = gsum[:].unsqueeze(2)
            own.after(v.tensor_copy(best, top[:, :, 0:1]))
            v.tensor_tensor(top, top, best.to_broadcast([P, PH * TB, TOPK]), ALU.subtract).then_inc(top_shift, 1)
            dve.wait_ge(gate_exp, 1)
            own.after(v.tensor_reduce(gsum[:], top, AX.X, ALU.add))
            own.after(v.reciprocal(grec[:], gsum[:]))
            v.tensor_tensor(top, top, grec[:].unsqueeze(2).to_broadcast([P, PH * TB, TOPK]), ALU.mult)\
                .then_inc(sel_ready, 1)

            def bodies(t):
                return t.rearrange("p (b t) -> p b t", t=TOK)

            dve.wait_ge(selT_done, 1)
            v.tensor_copy(selT[:, :, 0], bodies(bank[:, 6])).then_inc(sel_used, 1)
            dve.wait_ge(selT_done, 2)
            v.tensor_copy(selT[:, :, 1], bodies(bank[:, 7])).then_inc(sel_used, 1)
            dve.wait_ge(selT_done, 3)
            v.tensor_copy(gateT[:], bank[:, 6]).then_inc(sel_used, 1)
            dve.wait_ge(sel_used, 3)
            own.after(v.tensor_copy(gpart[:], gateT[:]))
            own.after(v.tensor_copy(selT[:, :, 2], bodies(gpart[:])))
            own.after(v.tensor_tensor(grest[:], gateT[:], gpart[:], ALU.subtract))
            own.after(v.tensor_copy(gpart[:], grest[:]))
            own.after(v.tensor_copy(selT[:, :, 3], bodies(gpart[:])))
            own.after(v.tensor_tensor(selT[:, :, 4], bodies(grest[:]), bodies(gpart[:]), ALU.subtract))

            def spread_out(i, s):
                def keys4(t):
                    return t.rearrange("p t (k j) -> p t k j", j=4)

                def value(which):
                    row = which * TOK + s * 8
                    return tok5[:, row:row + 8].unsqueeze(2).to_broadcast([P, 8, NKEY // 4, 4])

                keys = iota_b[:].rearrange("p (k j) -> p k j", j=4).unsqueeze(1).to_broadcast([P, 8, NKEY // 4, 4])
                dve.wait_ge(g_full, i * 4 + (2 * s + 1))
                own.after(v.tensor_tensor(keys4(hit[:, s]), keys, value(0), ALU.is_equal))
                v.tensor_tensor(keys4(onehot[:, s, 0]), keys, value(1), ALU.is_equal)
                for q in range(3):
                    ins = v.tensor_tensor(keys4(onehot[:, s, 1 + q]), keys4(hit[:, s]), value(2 + q), ALU.mult)
                ins.then_inc(onehot_done, 1)

            def a2_body(i, last):
                c = i * 2 + 64
                dve.wait_ge(onehot_done, i * 2 + 1)
                own.after(v.tensor_copy(tok5[:].unsqueeze(1),
                                        selT[:, bass.ds(i, 1)].rearrange("p o a t -> p o (a t)").unsqueeze(3)
                                        .to_broadcast([P, 1, 5 * TOK, 4])))
                spread_out(i, 0)
                split_lo(c + (N_A + 2), 0)
                spread_out(i, 1)
                if not last:
                    split_lo(c + (N_A + 3), 1)

            with own.repeat(31, 3) as i:
                a2_body(i, False)
            a2_body(31, True)

            def product(c, k, slot, e, landed):
                dve.wait_ge(gb_in[slot], landed)
                dve.wait_ge(hb_in[k], (c - k) * 8 + 16)
                dve.wait_ge(act_lo_done, c + 1)
                v.tensor_tensor(prod[:, k].rearrange("p (b t) -> p b t", t=TOK),
                                h_buf[:, k].rearrange("p (b t) -> p b t", t=TOK),
                                g_buf[:, slot, :, e].rearrange("p b e t -> p b (e t)"), ALU.mult)\
                    .then_inc(prod_done, 1)
                dve.wait_ge(act_hi_done, c + 1)
                v.tensor_tensor(act_lo[:, k], prod[:, k], act_hi[:, k].bitcast(F32), ALU.subtract)\
                    .then_inc(act_lo_done, 1)

            def b_eight(o, slot, last=False):
                def two(r, split):
                    for k in range(2):
                        c = o * 16 + r * 2 + (8 * slot + k)
                        product(c, k, slot, bass.ds(r * 2 + k, 1), o * 32 + 32)
                        if split:
                            split_lo(c + (N_B + 1), k + 1)

                with dve.Fori(0, 3 if last else 4) as r:
                    two(r, True)
                if last:
                    product(126, 0, slot, bass.ds(6, 1), 256)
                    split_lo(N_B + 127, 1)
                    product(127, 1, slot, bass.ds(7, 1), 256)

            with dve.Fori(0, 7) as o:
                b_eight(o, 0)
                b_eight(o, 1)
            b_eight(7, 0)
            b_eight(7, 1, last=True)

            dve.wait_ge(y_done, 1)
            for b in range(TB):
                for q in range(2):
                    half = h_sb[:, b, q * 512:(q + 1) * 512]
                    v.tensor_tensor(half, bank[:, 2 * b + q], half, ALU.add).then_inc(y_sum, 1)
            dve.wait_ge(y_sq, TB)
            own.after(rsqrt(D))
            for b in range(TB):
                v.scalar_tensor_tensor(o_sb[:, b], h_sb[:, b], rs_y[:, b:b + 1], gfin[:], ALU.mult, ALU.mult)\
                    .then_inc(o_ready, 1)

        @block.tensor
        def _(pe):
            def three(dst, a_hi, a_lo, b_hi, b_lo, start, stop, **kw):
                pe.matmul(dst, a_hi, b_hi, start=start, stop=False, **kw)
                pe.matmul(dst, a_hi, b_lo, start=False, stop=False, **kw)
                return pe.matmul(dst, a_lo, b_hi, start=False, stop=stop, **kw)

            def norm(k, tile):
                pe.wait_ge(n_x[k], TB)
                for c in range(DC):
                    for b in range(TB):
                        last = pe.transpose(bank[:, c, b * P:(b + 1) * P], tile[:, b, c * P:(c + 1) * P], ident[:])
                    last.then_inc(n_t[k], 1)
                pe.wait_ge(n_lo[k], DC)

            pe.wait_ge(const_in, 16 * 4)
            norm(0, x_sb)

            def section(n, par, rhs_hi=xT_hi, rhs_lo=xT_lo, free=bank_free, freed=0):
                s = par % 2
                pe.wait_ge(w_lo_done, n + 3)
                pe.wait_ge(free, n + (1 - freed))
                a_hi, a_lo = w_tile(w_hi, s), w_tile(w_lo, s)
                for c in range(DC):
                    last = three(bank[:, s], a_hi[:, c], a_lo[:, c], rhs_hi[:, c], rhs_lo[:, c], c == 0, c == DC - 1)
                last.then_inc(w_used, 1)

            def scores(U, u):
                s, nk = u % 2, (u + 1) * P
                pe.wait_ge(exp_done, U + 1)
                for m in range(2):
                    rows = slice(m * HD, (m + 1) * HD)
                    last = three(bank[:, 2 + 2 * s + m, 0:nk],
                                 qk_hi[rows, 0, u * P:nk], qk_lo[rows, 0, u * P:nk],
                                 qk_hi[rows, 1, 0:nk], qk_lo[rows, 1, 0:nk], True, True)
                last.then_inc(scores_done, 1)

            def t_wait(V):
                pe.wait_ge(t_lo, V + 1)

            def turn(U, V, u):
                pe.wait_ge(dif_ready, U + 3)
                t_wait(V)
                for c in range(u + 1):
                    last = pe.transpose(bank[:, 6, c * P:(c + 1) * P], dif[:, u % 2, c * P:(c + 1) * P], ident[:])
                last.then_inc(t_full, 1)

            def attend(U, V, u):
                pe.wait_ge(t_lo, V + 2)
                for c in range(u + 1):
                    last = three(bank[:, 7, u * P:(u + 1) * P], difT_hi[:, u % 2, c], difT_lo[:, u % 2, c],
                                 v_hi[:, c], v_lo[:, c], c == 0, c == u)
                last.then_inc(pv_done, 1)

            def l1_body(h, last):
                n = h * L1_BODY + L1_PRE
                U = h * 4
                V = h * 6
                section(n, 1)
                pe.wait_ge(bank_free, n + 2)
                t_wait(V)
                for b in range(TB):
                    ins = pe.transpose(bank[:, 6, b * P:(b + 1) * P], vT_sb[:, b * P:(b + 1) * P], ident[:])
                ins.then_inc(t_full, 1)
                pe.wait_ge(qk_ready, h * 2 + 3)
                scores(U, 0)
                scores(U + 1, 1)
                section(n + 1, 0)
                turn(U, V + 1, 0)
                scores(U + 2, 2)
                turn(U + 1, V + 2, 1)
                scores(U + 3, 3)
                section(n + 2, 1)
                pe.wait_ge(on_ready, h + 1)
                attend(U, V + 1, 0)
                turn(U + 2, V + 3, 2)
                attend(U + 1, V + 2, 1)
                turn(U + 3, V + 4, 3)
                if not last:
                    section(n + 3, 0)
                attend(U + 2, V + 3, 2)
                attend(U + 3, V + 4, 3)
                if not last:
                    section(n + 4, 1)
                pe.wait_ge(on_ready, h + 2)
                t_wait(V + 5)
                for u in range(TB):
                    ins = pe.transpose(bank[:, 6, u * P:(u + 1) * P], on_sb[:, u], ident[:])
                ins.then_inc(t_full, 1)
                if not last:
                    section(n + 5, 0)

            for n in range(L1_PRE):
                section(n, n)
            with pe.Fori(0, H - 1) as h:
                l1_body(h, False)
            l1_body(H - 1, True)

            def l2_body(i):
                n = i * 4 + N_L2
                section(n, 0)
                section(n + 1, 1)
                section(n + 2, 0, bzT_hi, bzT_lo)
                section(n + 3, 1, attnT_hi, attnT_lo)

            pe.wait_ge(bz_ready, H + 1)
            pe.wait_ge(t_lo, 6 * H + 1)
            with pe.Fori(0, DC) as i:
                l2_body(i)

            def add_rows(a_hi, a_lo, s, **kw):
                for b in range(TB):
                    for q in range(2):
                        cols = slice(q * 512, (q + 1) * 512)
                        last = three(bank[:, 2 * b + q], a_hi[:, b * P:(b + 1) * P], a_lo[:, b * P:(b + 1) * P],
                                     w_hi[:, s, cols], w_lo[:, s, cols], **kw)
                return last

            pe.wait_ge(mix_done, DC + 1)
            pe.wait_ge(bank_free, N_WO + 2)
            for c in range(DC):
                pe.wait_ge(w_lo_done, N_WO + c + 3)
                add_rows(mixT_hi[:, c], mixT_lo[:, c], c % 2, start=c == 0, stop=c == DC - 1).then_inc(w_used, 1)
            norm(1, xn_2)

            def key_scores(s, c):
                pe.wait_ge(q_done, s + 3)
                pe.wait_ge(key_lo, 1)
                pe.wait_ge(s_copied, s + 1)
                for b in range(TB):
                    toks = slice(b * P, (b + 1) * P)
                    last = three(bank[:, 2 + c, toks], q_hi[:, c, toks], q_lo[:, c, toks],
                                 keysT_hi[:, c], keysT_lo[:, c], True, True)
                last.then_inc(s_done, 1)

            def query(s, c):
                section(s + N_PQ, c, free=q_done, freed=N_PQ)

            query(0, 0)
            with pe.Fori(0, PH - 1) as h:
                s = h * 2
                query(s + 1, 1)
                key_scores(s, 0)
                query(s + 2, 0)
                key_scores(s + 1, 1)
            query(15, 1)
            key_scores(14, 0)
            key_scores(15, 1)
            pe.wait_ge(s_copied, 2 * PH + 2)

            def experts(c, k):
                pe.wait_ge(w_lo_done, c + (N_A + 3))
                pe.wait_ge(gel_done, c + 1)
                u_hi, u_lo = w_tile(w_hi, k), w_tile(w_lo, k)
                for q in range(DC):
                    last = three(bank[:, 4 + k], u_hi[:, q], u_lo[:, q], xT_hi[:, q], xT_lo[:, q],
                                 q == 0, q == DC - 1)
                last.then_inc(w_used, 1)

            def spread(i, j):
                if j % 2 == 0:
                    pe.wait_ge(onehot_done, i * 2 + (j // 2 + 2))
                pe.wait_ge(g_copied, i * 4 + (j + 1))
                for t in range(4):
                    own_t = j % 2 * 4 + t
                    for q in range(3):
                        last = pe.matmul(bank[:, 6 + j % 2, t * P:(t + 1) * P], onehot[:, j // 2, 0, own_t],
                                         onehot[:, j // 2, 1 + q, own_t], start=q == 0, stop=q == 2)
                last.then_inc(g_full, 1)

            with pe.Fori(0, 32) as i:
                experts(i * 2, 0)
                experts(i * 2 + 1, 1)
            pe.wait_ge(sel_ready, 1)
            for q in range(3):
                if q == 2:
                    pe.wait_ge(sel_used, 1)
                for b in range(TB):
                    last = pe.transpose(bank[:, 6 + q % 2, b * P:(b + 1) * P], sel[:, q, b].rearrange("p h k -> p (h k)"), ident[:])
                last.then_inc(selT_done, 1)
            pe.wait_ge(sel_used, 3)

            with pe.Fori(0, 32) as i:
                c = i * 2 + 64
                experts(c, 0)
                spread(i, 0)
                spread(i, 1)
                experts(c + 1, 1)
                spread(i, 2)
                spread(i, 3)

            pe.wait_ge(gel_done, NKEY + 2)
            pe.wait_ge(g_copied, T // 4 + 2)
            for q in range(8):
                pe.matmul(bank[:, q], zero_b[:, 0:P], zero_b[:], start=True, stop=False)
            with pe.Fori(0, NKEY // 2) as i:
                for k in range(2):
                    c = i * 2 + k
                    pe.wait_ge(act_lo_done, c + 3)
                    pe.wait_ge(w_lo_done, c + (N_B + 3))
                    add_rows(act_hi[:, k], act_lo[:, k], k, start=False, stop=False).then_inc(w_used, 1)
            for q in range(8):
                last = pe.matmul(bank[:, q], zero_b[:, 0:P], zero_b[:], start=False, stop=True)
            last.then_inc(y_done, 1)


def constants():
    import numpy as np
    f = np.float32
    inv = np.power(f(10000.0), -np.arange(0, HD, 2, dtype=f) / f(HD)).astype(f)
    ang = (np.arange(T, dtype=f)[None, :] * inv[:, None]).astype(f)
    cos, sin = np.cos(ang.astype(np.float64)).astype(f), np.sin(ang.astype(np.float64)).astype(f)
    row = np.arange(P)
    return {
        "c_cos": np.concatenate([cos] * 4),
        "c_sin": np.concatenate([-sin, sin] * 2),
        "c_ident": np.eye(P, dtype=f),
        "c_mask": np.where(row[None, :] <= row[:, None], f(0), f(-1e30)).astype(f),
        "c_iota": np.tile(row.astype(f), (P, 1)),
    }


def kernel(**inputs):
    import numpy as _np
    import concourse.bacc as _bacc
    from concourse import mybir as _mybir
    from concourse.bass_utils import run_bass_kernel_spmd as _run

    given = {name: _np.asarray(a) for name, a in inputs.items()}

    def tiles(w):
        return w.reshape(DC, P, -1, P).transpose(2, 1, 0, 3).reshape(-1, P, D)

    laid = {
        "x": given["x"],
        "norm_gains": _np.stack([given["norm1_g"][0], given["norm2_g"][0]]).reshape(2, DC, P).transpose(2, 0, 1),
        "w_in": tiles(given["w_in"][0]),
        "conv_w": given["conv_w"][0].reshape(KCONV, DC, P).transpose(2, 1, 0),
        "w_out_conv": tiles(given["w_out_conv"][0]),
        "lambdas": _np.stack([given[f"lambda_{n}"][0] for n in ("q1", "k1", "q2", "k2")]),
        "attn_subln_g": given["attn_subln_g"],
        "w_out_attn": tiles(given["w_out_attn"][0]),
        "w_o": given["w_o"],
        "peer_w_q": tiles(given["peer_w_q"][0]),
        "peer_keys": _np.stack([given["peer_keys1"][0].T, given["peer_keys2"][0].T], axis=1),
        "peer_u": tiles(given["peer_u"][0].T),
        "peer_v": given["peer_v"],
        "final_norm_g": given["final_norm_g"],
    }
    laid.update(constants())

    nc = _bacc.Bacc("TRN2", target_bir_lowering=False, num_devices=1)
    arrays, args = {}, []
    for name, value in laid.items():
        a = _np.ascontiguousarray(value)
        arrays[f"in_{name}"] = a
        args.append(nc.dram_tensor(f"in_{name}", a.shape, _mybir.dt.from_np(a.dtype), kind="ExternalInput").ap())
    args.append(nc.dram_tensor("out_0", (1, T, D), _mybir.dt.float32, kind="ExternalOutput").ap())
    peer_block(nc, *args)
    r = _run(nc, [arrays], core_ids=[0])
    return r.results[0]["out_0"]
```

```python
from contextlib import ExitStack, contextmanager

import concourse.bass as bass
from concourse import mybir

F32 = mybir.dt.float32
F32R = mybir.dt.float32r
BF16 = mybir.dt.bfloat16
I32 = mybir.dt.int32
U32 = mybir.dt.uint32
ACT = mybir.ActivationFunctionType
ALU = mybir.AluOpType
AX = mybir.AxisListType

P = 128
D = 1024
T = 512
DC = D // P
TB = T // P
H = 8
HD = D // (2 * H)
KCONV = 3
PH = 8
TOPK = 16
NKEY = 128
LAM_INIT = 0.8 - 0.6
SCALE = HD ** -0.5
EPS = 1e-6
LOW = -3.0e38
RSQRT_MAGIC = 0x5F3759DF

L1_PRE = 5
L1_BODY = 6
N_L2 = L1_BODY * H
N_WO = N_L2 + 4 * DC
N_PQ = N_WO + DC
N_A = N_PQ + 2 * PH
N_B = N_A + NKEY
N_END = N_B + NKEY
SECTION = {"b": 0, "c": 1, "u": 2, "q": 3, "k": 4, "v": 5, "gc": 6, "ga": 7}
TOK = 16
BODIES = T // TOK


class Steps:

    def __init__(self, eng, sem):
        self.eng, self.sem, self.base, self.k, self.loops = eng, sem, 0, 0, []

    def value(self):
        v = self.base + self.k
        for i, per in self.loops:
            v = i * per + v
        return v

    def after(self, ins):
        self.end(ins)
        self.wait()

    def end(self, ins):
        ins.then_inc(self.sem, 1)
        self.k += 1

    def wait(self):
        self.eng.wait_ge(self.sem, self.value())

    @contextmanager
    def repeat(self, count, per):
        base, k = self.base, self.k
        with self.eng.Fori(0, count) as i:
            self.base, self.k = base + k, 0
            self.loops.append((i, per))
            yield i
            assert self.k == per, (self.k, per)
            self.loops.pop()
        self.base, self.k = base + k + count * per, 0


def peer_block(nc, x, norm_gains, w_in, conv_w, w_out_conv, lambdas, attn_subln_g, w_out_attn, w_o, peer_w_q,
               peer_keys, peer_u, peer_v, final_norm_g, c_cos, c_sin, c_ident, c_mask, c_iota, out):
    gel_dram = nc.dram_tensor("gelu_spill", (NKEY, P, T), F32, kind="Internal").ap()
    gate_dram = nc.dram_tensor("gate_spill", (BODIES, P, NKEY, TOK), F32, kind="Internal").ap()

    wo_v = w_o[0].rearrange("(c p) n -> c p n", p=P)
    v_v = peer_v[0].rearrange("(c p) d -> c p d", p=P)
    x_v = x[0].rearrange("(b p) d -> p b d", p=P)
    out_v = out[0].rearrange("(b p) d -> b p d", p=P)

    ctx = ExitStack()
    with ctx:
        def sem(name):
            return ctx.enter_context(nc.semaphore(name))

        def space(stack):
            return lambda name, shape, dt=F32: stack.enter_context(nc.sbuf_tensor(name, shape, dt))

        sb = space(ctx)
        ident = sb("ident", [P, P])
        iota_f = sb("iota_f", [P, P])
        iota_b = sb("iota_b", [P, P], BF16)
        zero_b = sb("zero_b", [P, T], BF16)
        norm_g = sb("norm_g", [P, 2, DC])
        gfin = sb("gfin", [P, D])
        xT_hi = sb("xT_hi", [P, DC, T], F32R)
        xT_lo = sb("xT_lo", [P, DC, T], F32R)
        w_raw = sb("w_raw", [P, 2, D])
        w_hi = sb("w_hi", [P, 2, D], F32R)
        w_lo = sb("w_lo", [P, 2, D], F32R)
        keysT_hi = sb("keysT_hi", [P, 2, NKEY], F32R)
        keysT_lo = sb("keysT_lo", [P, 2, NKEY], F32R)
        stat = sb("stat", [P, 4])
        rs_a = sb("rs_a", [P, 4])
        rs_i = sb("rs_i", [P, 4], I32)
        rs_t = sb("rs_t", [P, 4])
        rs_y = sb("rs_y", [P, 4])
        junk = sb("junk", [P, D])

        s0 = ExitStack()
        a = space(s0)
        x_sb = a("x_sb", [P, TB, D])
        keys_sb = a("keys_sb", [P, 2, NKEY])
        s0.close()
        sL = ExitStack()
        a = space(sL)
        attnT_hi = a("attnT_hi", [P, H, T], F32R)
        attnT_lo = a("attnT_lo", [P, H, T], F32R)
        bzT_hi = a("bzT_hi", [P, DC, T], F32R)
        bzT_lo = a("bzT_lo", [P, DC, T], F32R)
        sgc = a("sgc", [P, T])
        sga = a("sga", [P, T])
        yc_sb = a("yc_sb", [P, T])
        s1 = ExitStack()
        a = space(s1)
        cos_t = a("cos_t", [P, T])
        sin_t = a("sin_t", [P, T])
        mask_t = a("mask_t", [P, P])
        mask_b = a("mask_b", [P, P], BF16)
        ident_b = a("ident_b", [P, P], BF16)
        cw = a("cw", [P, DC, KCONV])
        cw_h = a("cw_h", [P, KCONV])
        subln_g = a("subln_g", [P, 1])
        lam4 = a("lam4", [P, 4, HD])
        lam_p = a("lam_p", [P, 2, HD])
        lam_s = a("lam_s", [P, 2])
        neg_lam = a("neg_lam", [P, 1])
        qk_raw = a("qk_raw", [P, 2, T])
        qk_rot = a("qk_rot", [P, 2, T])
        rope_a = a("rope_a", [P, T])
        rope_b = a("rope_b", [P, T])
        qk_hi = a("qk_hi", [P, 2, T], F32R)
        qk_lo = a("qk_lo", [P, 2, T], F32R)
        vT_sb = a("vT_sb", [P, T])
        v_hi = a("v_hi", [P, TB, P], F32R)
        v_lo = a("v_lo", [P, TB, P], F32R)
        c_sb = a("c_sb", [P, T])
        u_sb = a("u_sb", [P, T])
        b_sb = a("b_sb", [P, T])
        cu = a("cu", [P, T + KCONV - 1])
        z_a = a("z_a", [P, T])
        z_b = a("z_b", [P, T])
        nbias = a("nbias", [P, 2, 2])
        prob = a("prob", [P, 2, 2, T])
        zsum = a("zsum", [P, 2, 2])
        rz = a("rz", [P, 2, 2])
        p1s = a("p1s", [P, T])
        dif = a("dif", [P, P * (1 + 2 + 3 + 4)])
        difT_hi = a("difT_hi", [P, TB + 3, P], F32R)
        difT_lo = a("difT_lo", [P, TB + 3, P], F32R)
        on_sb = a("on_sb", [P, TB, P])
        s1.close()
        s2 = ExitStack()
        a = space(s2)
        mixT_hi = a("mixT_hi", [P, DC, T], F32R)
        mixT_lo = a("mixT_lo", [P, DC, T], F32R)
        ya_sb = a("ya_sb", [P, T])
        m_a = a("m_a", [P, T])
        m_b = a("m_b", [P, T])
        m_c = a("m_c", [P, T])
        s2.close()
        sL.close()
        h_sb = sb("h_sb", [P, TB, D])
        sN = ExitStack()
        xn_2 = space(sN)("xn_2", [P, TB, D])
        sN.close()
        sP = ExitStack()
        a = space(sP)
        score = a("score", [P, TB, PH, 2, NKEY])
        q_hi = a("q_hi", [P, 2, T], F32R)
        q_lo = a("q_lo", [P, 2, T], F32R)
        gel = a("gel", [P, 2, T])
        sw = a("sw", [P, 2, NKEY])
        sw2 = a("sw2", [P, 2, NKEY])
        tval = a("tval", [P, 2, TOPK])
        tidx = a("tidx", [P, 2, TOPK], U32)
        tidx_b = a("tidx_b", [P, 2, TOPK], BF16)
        cand = a("cand", [P, TOPK, TOPK])
        cand2 = a("cand2", [P, TOPK * TOPK])
        cval = a("cval", [P, TOPK])
        cidx = a("cidx", [P, TOPK], U32)
        crank = a("crank", [P, 2, TOPK], U32)
        crank_b = a("crank_b", [P, 2 * TOPK, 2], BF16)
        pick = a("pick", [P, 2 * TOPK, TOPK], BF16)
        pick2 = a("pick2", [P, 2 * TOPK, TOPK], BF16)
        sel = a("sel", [P, 3, TB, PH, TOPK])
        gsum = a("gsum", [P, PH * TB])
        grec = a("grec", [P, PH * TB])
        selT = a("selT", [P, BODIES, 5, TOK])
        gpart = a("gpart", [P, T], BF16)
        grest = a("grest", [P, T])
        gateT = a("gateT", [P, T])
        tok5 = a("tok5", [P, 5 * TOK, 4], BF16)
        hit = a("hit", [P, 2, 8, NKEY], BF16)
        onehot = a("onehot", [P, 2, 4, 8, NKEY], BF16)
        g_stage = a("g_stage", [P, NKEY, TOK])
        sP.close()
        sB = ExitStack()
        a = space(sB)
        g_buf = a("g_buf", [P, 2, BODIES, 8, TOK])
        h_buf = a("h_buf", [P, 2, T])
        prod = a("prod", [P, 2, T])
        act_hi = a("act_hi", [P, 2, T], F32R)
        act_lo = a("act_lo", [P, 2, T], F32R)
        o_sb = a("o_sb", [P, TB, D])
        sB.close()

        bank = ctx.enter_context(nc.psum_tensor("bank", [P, 8, 512], F32))

        const_in = sem("const_in")
        x_in = sem("x_in")
        key_in = sem("key_in")
        consts_out = sem("consts_out")
        key_hi = sem("key_hi")
        key_lo = sem("key_lo")
        lam_exp = sem("lam_exp")
        lam_dot = sem("lam_dot")
        w_in_sem = [sem("w_landed0"), sem("w_landed1")]
        w_hi_done = sem("w_hi_done")
        w_lo_done = sem("w_lo_done")
        w_used = sem("w_used")
        bank_free = sem("bank_free")
        dve_own = sem("dve_own")
        n_sq = [sem(f"n{k}_squares") for k in (1, 2)]
        n_x = [sem(f"n{k}_scaled") for k in (1, 2)]
        n_t = [sem(f"n{k}_transposed") for k in (1, 2)]
        n_hi = [sem(f"n{k}_hi") for k in (1, 2)]
        n_lo = [sem(f"n{k}_lo") for k in (1, 2)]
        mask_ready = sem("mask_ready")
        qk_ready = sem("qk_ready")
        cu_ready = sem("cu_ready")
        bz_ready = sem("bz_ready")
        scores_done = sem("scores_done")
        bias_ready = sem("bias_ready")
        exp_done = sem("exp_done")
        dif_ready = sem("dif_ready")
        t_full = sem("t_full")
        t_hi = sem("t_hi")
        t_lo = sem("t_lo")
        pv_done = sem("pv_done")
        o_squares = sem("o_squares")
        o_scale = sem("o_scale")
        on_ready = sem("on_ready")
        half_mix = sem("half_mix")
        mix_done = sem("mix_done")
        h_ready = sem("h_ready")
        q_hi_done = sem("q_hi_done")
        q_done = sem("q_done")
        s_done = sem("s_done")
        s_copied = sem("s_copied")
        gel_done = sem("gel_done")
        gel_out = [sem("gel_stored0"), sem("gel_stored1")]
        top_shift = sem("top_shift")
        gate_exp = sem("gate_exp")
        sel_ready = sem("sel_ready")
        sel_used = sem("sel_used")
        selT_done = sem("selT_done")
        onehot_done = sem("onehot_done")
        g_full = sem("g_full")
        g_copied = sem("g_copied")
        g_out = sem("g_stored")
        gb_in = [sem("gates_landed0"), sem("gates_landed1")]
        hb_in = [sem("gelu_landed0"), sem("gelu_landed1")]
        prod_done = sem("prod_done")
        act_hi_done = sem("act_hi_done")
        act_lo_done = sem("act_lo_done")
        y_done = sem("y_done")
        y_sum = sem("y_sum")
        y_sq = sem("y_squares")
        o_ready = sem("o_ready")
        stored = sem("stored")

        block = ctx.enter_context(nc.Block())

        def w_tile(t, n):
            return t[:, n % 2, :].rearrange("p (c n) -> p c n", c=DC)

        @block.sync
        def _(sp):
            sp.dma_start(x_sb[:], x_v).then_inc(x_in, 16)
            sp.dma_start(ident[:], c_ident).then_inc(const_in, 16)
            sp.dma_start(iota_f[:], c_iota).then_inc(const_in, 16)
            sp.dma_start(norm_g[:], norm_gains).then_inc(const_in, 16)
            sp.dma_start(gfin[:], final_norm_g.partition_broadcast(P)).then_inc(const_in, 16)
            sp.dma_start(keys_sb[:], peer_keys).then_inc(key_in, 16)

            def load(n, par, src):
                sp.wait_ge(w_lo_done, n + 1)
                s = par % 2
                sp.dma_start(w_raw[:, s, :], src).then_inc(w_in_sem[s], 16)

            def section(name, h):
                return w_in[bass.ds(h + SECTION[name] * DC, 1)]

            for n, name in enumerate("qk"):
                load(n, n, section(name, 0))
            sp.dma_start(cos_t[:], c_cos).then_inc(consts_out, 16)
            sp.dma_start(sin_t[:], c_sin).then_inc(consts_out, 16)
            sp.dma_start(mask_t[:], c_mask).then_inc(consts_out, 16)
            sp.dma_start(cw[:], conv_w).then_inc(consts_out, 16)
            sp.dma_start(subln_g[:], attn_subln_g[0].rearrange("(p a) -> p a", a=1)).then_inc(consts_out, 16)
            sp.dma_start(lam4[:], lambdas.partition_broadcast(P)).then_inc(consts_out, 16)
            for n, name in enumerate("vcu"):
                load(2 + n, n, section(name, 0))
            with sp.Fori(0, H - 1) as h:
                n = h * L1_BODY + L1_PRE
                load(n, 1, section("b", h))
                for j, name in enumerate("qkvcu"):
                    load(n + (1 + j), j, section(name, h + 1))
            load(N_L2 - 1, 1, section("b", H - 1))
            load(N_L2, 0, section("gc", 0))
            load(N_L2 + 1, 1, section("ga", 0))
            load(N_L2 + 2, 0, w_out_conv[0])
            with sp.Fori(0, DC - 1) as i:
                n = i * 4 + (N_L2 + 3)
                load(n, 1, section("gc", i + 1))
                load(n + 1, 0, w_out_attn[bass.ds(i, 1)])
                load(n + 2, 1, section("ga", i + 1))
                load(n + 3, 0, w_out_conv[bass.ds(i + 1, 1)])
            load(N_WO - 1, 1, w_out_attn[DC - 1])
            for c in range(DC):
                load(N_WO + c, N_WO + c, wo_v[c])
                if c == 1:
                    sp.wait_ge(w_used, N_WO + 2)
                    sp.dma_start(h_sb[:], x_v).then_inc(x_in, 16)
            with sp.Fori(0, PH) as h:
                for c in range(2):
                    load(h * 2 + (N_PQ + c), N_PQ + c, peer_w_q[bass.ds(h * 2 + c, 1)])

            for c in range(2):
                load(N_A + c, N_A + c, peer_u[c])

            def a_chunk(c, k, src):
                load(c + (N_A + 2), k, src)
                sp.wait_ge(gel_done, c + 3)
                sp.dma_start(gel_dram[bass.ds(c, 1)], gel[:, k]).then_inc(gel_out[k], 16)

            def a2_store(i):
                sp.wait_ge(g_copied, i * 4 + 6)
                sp.dma_start(gate_dram[bass.ds(i, 1)], g_stage[:]).then_inc(g_out, 16)

            with sp.Fori(0, 32) as i:
                for k in range(2):
                    a_chunk(i * 2 + k, k, peer_u[bass.ds(i * 2 + (2 + k), 1)])
            with sp.Fori(0, 31) as i:
                for k in range(2):
                    a_chunk(i * 2 + (64 + k), k, peer_u[bass.ds(i * 2 + (66 + k), 1)])
                a2_store(i)
            for k in range(2):
                a_chunk(126 + k, k, v_v[k])
            a2_store(31)

            for k in range(2):
                sp.wait_ge(gel_out[k], 16 * 65)
            sp.wait_ge(g_out, 16 * (BODIES + 1))
            sp.wait_ge(g_full, T // 4 + 3)

            def gates(block_of_8, s):
                src = gate_dram[:, :, bass.ds(block_of_8 * 8, 8), :].rearrange("b p e t -> p b e t")
                for q in range(2):
                    sp.dma_start(g_buf[:, s, q * (BODIES // 2):(q + 1) * (BODIES // 2)],
                                 src[:, q * (BODIES // 2):(q + 1) * (BODIES // 2)]).then_inc(gb_in[s], 16)

            def gelus(c, k):
                sp.dma_start(h_buf[:, k], gel_dram[bass.ds(c, 1)]).then_inc(hb_in[k], 16)

            for s in range(2):
                gates(s, s)
            for k in range(2):
                gelus(k, k)

            def b_chunks(c, last=False):
                for k in range(2):
                    load(c + (N_B + 2 + k), k, v_v[bass.ds(c + (2 + k), 1)])
                    sp.wait_ge(prod_done, c + (3 + k))
                    gelus(c + (2 + k), k)

            with sp.Fori(0, 7) as o:
                for s in range(2):
                    with sp.Fori(0, 4) as r:
                        b_chunks(o * 16 + r * 2 + 8 * s)
                    sp.wait_ge(prod_done, o * 16 + (8 * s + 10))
                    gates(o * 2 + (2 + s), s)
            with sp.Fori(0, 7) as r:
                b_chunks(r * 2 + 112)
            for b in range(TB):
                sp.wait_ge(o_ready, b + 1)
                sp.dma_start(out_v[b], o_sb[:, b]).then_inc(stored, 16)
            sp.wait_ge(stored, 16 * TB)

        @block.gpsimd
        def _(pool):
            for s, n in ((w_lo_done, 2), (w_used, 2), (bank_free, 2), (bz_ready, 1),
                         (exp_done, 2), (dif_ready, 2), (t_lo, 1), (pv_done, 2), (on_ready, 1), (o_squares, 1), (qk_ready, 1),
                         (mix_done, 1), (q_done, 2), (s_done, 2), (s_copied, 2), (gel_done, 2), (gel_out[0], 16), (gel_out[1], 16),
                         (g_full, 3), (g_copied, 2), (g_out, 16), (prod_done, 2), (act_lo_done, 2), (onehot_done, 1)):
                pool.sem_inc(s, n)

        @block.scalar
        def _(act):
            def copy(dst, src, **kw):
                return act.activation(dst, src, ACT.Copy, **kw)

            def split_hi(n, par):
                s = par % 2
                act.wait_ge(w_in_sem[s], (n - s) * 8 + 16)
                act.wait_ge(w_used, n + 1)
                copy(w_hi[:, s, :], w_raw[:, s, :]).then_inc(w_hi_done, 1)

            def norm(k, src, ready):
                for b in range(TB):
                    ready(b)
                    if b:
                        act.wait_ge(n_sq[k], b)
                    act.activation(junk[:], src[:, b], ACT.Square, accum_out=stat[:, b:b + 1]).then_inc(n_sq[k], 1)
                if k == 0:
                    act.wait_ge(key_in, 16)
                    copy(keysT_hi[:], keys_sb[:]).then_inc(key_hi, 1)
                for c in range(DC):
                    act.wait_ge(n_t[k], c + 1)
                    copy(xT_hi[:, c], bank[:, c], scale=norm_g[:, k, c:c + 1]).then_inc(n_hi[k], 1)

            act.wait_ge(x_in, 16)
            act.wait_ge(const_in, 16 * 4)
            norm(0, x_sb, lambda b: None)
            split_hi(0, 0)
            split_hi(1, 1)
            act.wait_ge(lam_dot, 2)
            act.activation(lam_s[:], lam_s[:], ACT.Exp).then_inc(lam_exp, 1)

            def evac(n, par):
                act.wait_ge(w_used, n + 3)
                return bank[:, par % 2]

            def out_qk(n, par, which, h, first=False):
                src = evac(n, par)
                if not first:
                    act.wait_ge(qk_ready, h * 2 + which)
                scale = 1.0 if which else SCALE
                copy(qk_raw[:, which], src, scale=scale)
                for q in range(4):
                    d = q ^ 1
                    last = copy(qk_rot[32 * d:32 * d + 32, which], src[32 * q:32 * q + 32], scale=scale)
                last.then_inc(bank_free, 1)

            def t_out(v, dst, scale=None):
                act.wait_ge(t_full, v + 1)
                n = dst.shape[1]
                src = bank[:, 6, 0:n * P].rearrange("p (c n) -> p c n", c=n)
                kw = {} if scale is None else {"scale": scale}
                copy(dst, src, **kw).then_inc(t_hi, 1)

            def exps(U, u):
                sp_, nk = u % 2, (u + 1) * P
                act.wait_ge(bias_ready, U + 1)
                act.wait_ge(dif_ready, U + 1)
                for m in range(2):
                    ins = act.activation(prob[:, sp_, m, 0:nk], bank[:, 2 + 2 * sp_ + m, 0:nk], ACT.Exp,
                                         bias=nbias[:, sp_, m:m + 1],
                                         accum_out=zsum[:, sp_, m:m + 1])
                ins.then_inc(exp_done, 1)

            def squares(U, u):
                act.wait_ge(o_squares, U + 1)
                act.activation(junk[:, 0:P], bank[:, 7, u * P:(u + 1) * P], ACT.Square,
                               accum_out=stat[:, u:u + 1]).then_inc(o_squares, 1)

            def first_scores(n, U, V, h=None):
                if h is not None:
                    act.wait_ge(cu_ready, h + 1)
                copy(c_sb[:], evac(n, 1)).then_inc(bank_free, 1)
                split_hi(n + 2, 1)
                t_out(V, v_hi[:])
                exps(U, 0)
                exps(U + 1, 1)
                copy(u_sb[:], evac(n + 1, 0)).then_inc(bank_free, 1)
                split_hi(n + 3, 0)

            def l1_body(h, last):
                n = h * L1_BODY + L1_PRE
                U = h * 4
                V = h * 5
                exps(U + 2, 2)
                exps(U + 3, 3)
                act.wait_ge(bz_ready, h + 1)
                copy(b_sb[:], evac(n, 1)).then_inc(bank_free, 1)
                split_hi(n + 2, 1)
                act.wait_ge(pv_done, U + 2)
                t_out(V + 1, difT_hi[:, 0:3])
                if last:
                    act.activation(sgc[:], evac(n + 1, 0), ACT.Sigmoid).then_inc(bank_free, 1)
                else:
                    out_qk(n + 1, 0, 0, h + 1)
                split_hi(n + 3, 0)
                act.wait_ge(pv_done, U + 1)
                t_out(V + 2, difT_hi[:, TB:TB + 3])
                if last:
                    act.activation(sga[:], evac(n + 2, 1), ACT.Sigmoid).then_inc(bank_free, 1)
                else:
                    out_qk(n + 2, 1, 1, h + 1)
                split_hi(n + 4, 1)
                act.wait_ge(pv_done, U + 4)
                t_out(V + 3, difT_hi[:, 0:TB])
                copy(yc_sb[:] if last else vT_sb[:], evac(n + 3, 0)).then_inc(bank_free, 1)
                split_hi(n + 5, 0)
                act.wait_ge(pv_done, U + TB + 2)
                for u in range(TB):
                    squares(U + u, u)
                act.wait_ge(o_scale, h + 1)
                for u in range(TB):
                    ins = copy(on_sb[:, u], bank[:, 7, u * P:(u + 1) * P], scale=rs_y[:, u:u + 1])
                ins.then_inc(on_ready, 1)
                if not last:
                    first_scores(n + 4, U + 4, V + 4, h)
                v_on = V + (4 if last else 5)
                act.wait_ge(t_full, v_on + 1)
                copy(attnT_hi[:, bass.ds(h, 1)], bank[:, 6].unsqueeze(1), scale=subln_g[:, 0:1]).then_inc(t_hi, 1)

            act.wait_ge(consts_out, 16 * 6)
            out_qk(0, 0, 0, 0, first=True)
            split_hi(2, 0)
            out_qk(1, 1, 1, 0, first=True)
            split_hi(3, 1)
            copy(vT_sb[:], evac(2, 0)).then_inc(bank_free, 1)
            split_hi(4, 0)
            first_scores(3, 0, 0)
            with act.Fori(0, H - 1) as h:
                l1_body(h, False)
            l1_body(H - 1, True)

            with act.Fori(0, DC - 1) as i:
                n = i * 4 + (N_L2 + 3)
                act.wait_ge(half_mix, i + 1)
                act.activation(sgc[:], evac(n, 1), ACT.Sigmoid).then_inc(bank_free, 1)
                split_hi(n + 2, 1)
                act.wait_ge(mix_done, i + 1)
                copy(ya_sb[:], evac(n + 1, 0)).then_inc(bank_free, 1)
                split_hi(n + 3, 0)
                act.wait_ge(mix_done, i + 2)
                act.activation(sga[:], evac(n + 2, 1), ACT.Sigmoid).then_inc(bank_free, 1)
                split_hi(n + 4, 1)
                copy(yc_sb[:], evac(n + 3, 0)).then_inc(bank_free, 1)
                split_hi(n + 5, 0)
            act.wait_ge(mix_done, DC)
            copy(ya_sb[:], evac(N_WO - 1, 1)).then_inc(bank_free, 1)
            split_hi(N_WO + 1, 1)
            for c in range(DC):
                split_hi(N_WO + c + 2, c)
            norm(1, h_sb, lambda b: act.wait_ge(h_ready, 2 * b + 2))

            def q_out(s, c):
                act.wait_ge(w_used, s + (N_PQ + 3))
                act.wait_ge(s_done, s + 1)
                copy(q_hi[:, c], bank[:, c]).then_inc(q_hi_done, 1)

            def s_out(h, s, c):
                act.wait_ge(s_done, s + 3)
                copy(score[:, :, bass.ds(h, 1), c],
                     bank[:, 2 + c].rearrange("p (b a n) -> p b a n", a=1, b=TB)).then_inc(s_copied, 1)

            q_out(0, 0)
            split_hi(N_PQ + 2, 0)
            with act.Fori(0, PH - 1) as h:
                s = h * 2
                q_out(s + 1, 1)
                split_hi(s + (N_PQ + 3), 1)
                s_out(h, s, 0)
                q_out(s + 2, 0)
                split_hi(s + (N_PQ + 4), 0)
                s_out(h, s + 1, 1)
            q_out(15, 1)
            split_hi(N_PQ + 17, 1)
            s_out(PH - 1, 14, 0)
            s_out(PH - 1, 15, 1)

            def gelu(c, k, split=True):
                act.wait_ge(w_used, c + (N_A + 3))
                act.wait_ge(gel_out[k], (c - k) * 8 + 16)
                act.activation(gel[:, k], bank[:, 4 + k], ACT.Gelu).then_inc(gel_done, 1)
                if split:
                    split_hi(c + (N_A + 2), k)

            def g_group(g, slot, k):
                act.wait_ge(g_full, g + 4)
                copy(g_stage[:, :, 4 * k:4 * k + 4], bank[:, 6 + slot].rearrange("p (t e) -> p e t", t=4))\
                    .then_inc(g_copied, 1)

            with act.Fori(0, 32) as i:
                gelu(i * 2, 0)
                gelu(i * 2 + 1, 1)
            act.wait_ge(top_shift, 1)
            act.activation(sel[:, 2], sel[:, 2], ACT.Exp).then_inc(gate_exp, 1)

            def a2_body(i, last):
                c = i * 2 + 64
                gelu(c, 0)
                act.wait_ge(g_out, i * 16 + 16)
                g_group(i * 4, 0, 0)
                g_group(i * 4 + 1, 1, 1)
                gelu(c + 1, 1, split=not last)
                g_group(i * 4 + 2, 0, 2)
                g_group(i * 4 + 3, 1, 3)

            with act.Fori(0, 31) as i:
                a2_body(i, False)
            a2_body(31, True)

            def b_chunk(c, k, split=True):
                act.wait_ge(prod_done, c + 3)
                act.wait_ge(w_used, c + (N_B + 1))
                copy(act_hi[:, k], prod[:, k]).then_inc(act_hi_done, 1)
                if split:
                    split_hi(c + (N_B + 1), k + 1)

            with act.Fori(0, 63) as i:
                for k in range(2):
                    b_chunk(i * 2 + k, k)
            b_chunk(126, 0)
            b_chunk(127, 1, split=False)
            for b in range(TB):
                act.wait_ge(y_sum, 2 * b + 2)
                if b:
                    act.wait_ge(y_sq, b)
                act.activation(junk[:], h_sb[:, b], ACT.Square, accum_out=stat[:, b:b + 1]).then_inc(y_sq, 1)

        @block.vector
        def _(dve):
            v = nc.vector
            own = Steps(dve, dve_own)

            def split_lo(n, par):
                s = par % 2
                dve.wait_ge(w_hi_done, n + 1)
                v.tensor_tensor(w_lo[:, s, :], w_raw[:, s, :], w_hi[:, s, :].bitcast(F32), ALU.subtract)\
                    .then_inc(w_lo_done, 1)

            def rsqrt(width):
                own.after(v.tensor_scalar(rs_a[:], stat[:], 1.0 / width, EPS, ALU.mult, ALU.add))
                own.after(v.tensor_single_scalar(rs_i[:], rs_a[:].bitcast(I32), 1, ALU.arith_shift_right))
                own.after(v.tensor_scalar(rs_y[:].bitcast(I32), rs_i[:], -1.0, float(RSQRT_MAGIC), ALU.mult, ALU.add))
                for k in range(3):
                    own.after(v.scalar_tensor_tensor(rs_t[:], rs_y[:], -0.5, rs_y[:], ALU.mult, ALU.mult))
                    own.after(v.tensor_tensor(rs_t[:], rs_t[:], rs_a[:], ALU.mult))
                    ins = v.scalar_tensor_tensor(rs_y[:], rs_t[:], 1.5, rs_y[:], ALU.add, ALU.mult)
                    if k < 2:
                        own.after(ins)
                return ins

            def norm(k, src, tile):
                dve.wait_ge(n_sq[k], TB)
                own.after(rsqrt(D))
                for b in range(TB):
                    v.tensor_scalar(tile[:, b], src[:, b], rs_y[:, b:b + 1], None, ALU.mult).then_inc(n_x[k], 1)
                for c in range(DC):
                    dve.wait_ge(n_hi[k], c + 1)
                    v.scalar_tensor_tensor(xT_lo[:, c], bank[:, c], norm_g[:, k, c:c + 1],
                                           xT_hi[:, c].bitcast(F32), ALU.mult, ALU.subtract).then_inc(n_lo[k], 1)

            v.memset(zero_b[:], 0.0)
            dve.wait_ge(const_in, 16 * 4)
            v.tensor_copy(iota_b[:], iota_f[:])
            v.tensor_copy(ident_b[:], ident[:]).then_inc(mask_ready, 1)
            dve.wait_ge(key_hi, 1)
            v.tensor_tensor(keysT_lo[:], keys_sb[:], keysT_hi[:].bitcast(F32), ALU.subtract).then_inc(key_lo, 1)
            norm(0, x_sb, x_sb)
            split_lo(0, 0)
            split_lo(1, 1)
            dve.wait_ge(consts_out, 16 * 6)
            own.after(v.tensor_tensor(lam_p[:, 0], lam4[:, 0], lam4[:, 1], ALU.mult))
            own.after(v.tensor_tensor(lam_p[:, 1], lam4[:, 2], lam4[:, 3], ALU.mult))
            for k in range(2):
                v.tensor_reduce(lam_s[:, k:k + 1], lam_p[:, k], AX.X, ALU.add).then_inc(lam_dot, 1)
            v.tensor_copy(mask_b[:], mask_t[:]).then_inc(mask_ready, 1)
            own.after(v.memset(cu[:, 0:KCONV - 1], 0.0))
            own.after(v.tensor_scalar(subln_g[:], subln_g[:], 1.0 - LAM_INIT, None, ALU.mult))
            dve.wait_ge(lam_exp, 1)
            own.after(v.tensor_tensor(neg_lam[:], lam_s[:, 1:2], lam_s[:, 0:1], ALU.subtract))
            own.after(v.tensor_scalar(neg_lam[:], neg_lam[:], -LAM_INIT, None, ALU.add))

            def rope(n, which, h):
                dve.wait_ge(bank_free, n + 3)
                dve.wait_ge(qk_ready, h * 2 + (which + 1))
                own.end(v.tensor_tensor(rope_a[:], qk_raw[:, which], cos_t[:], ALU.mult))
                own.after(v.tensor_tensor(rope_b[:], qk_rot[:, which], sin_t[:], ALU.mult))
                own.after(v.tensor_tensor(rope_a[:], rope_a[:], rope_b[:], ALU.add))
                own.after(v.tensor_copy(qk_hi[:, which], rope_a[:]))
                v.tensor_tensor(qk_lo[:, which], rope_a[:], qk_hi[:, which].bitcast(F32), ALU.subtract)\
                    .then_inc(qk_ready, 1)

            def t_out(V, hi, lo):
                dve.wait_ge(t_hi, V + 1)
                n = hi.shape[1]
                src = bank[:, 6, 0:n * P].rearrange("p (c n) -> p c n", c=n)
                v.tensor_tensor(lo, src, hi.bitcast(F32), ALU.subtract).then_inc(t_lo, 1)

            def row_max(U, u):
                s, nk = u % 2, (u + 1) * P
                dve.wait_ge(scores_done, U + 1)
                v.tensor_reduce(nbias[:, s], bank[:, 2 + 2 * s:4 + 2 * s, 0:nk], AX.X, ALU.max, negate=True)\
                    .then_inc(bias_ready, 1)

            def combine(U, u):
                s, nk = u % 2, (u + 1) * P
                at = P * (u * (u + 1) // 2)
                dve.wait_ge(exp_done, U + 3)
                own.after(v.reciprocal(rz[:, s], zsum[:, s]))
                own.after(v.tensor_scalar(p1s[:, 0:nk], prob[:, s, 1, 0:nk], rz[:, s, 1:2], neg_lam[:, 0:1],
                                          ALU.mult, ALU.mult))
                v.scalar_tensor_tensor(dif[:, at:at + nk], prob[:, s, 0, 0:nk], rz[:, s, 0:1], p1s[:, 0:nk],
                                       ALU.mult, ALU.add).then_inc(dif_ready, 1)

            def first_scores(n, U, V):
                split_lo(n + 2, 1)
                t_out(V, v_hi[:], v_lo[:])
                row_max(U, 0)
                row_max(U + 1, 1)
                combine(U, 0)
                combine(U + 1, 1)
                split_lo(n + 3, 0)
                dve.wait_ge(bank_free, n + 4)
                v.tensor_tensor(cu[:, 2:2 + T], c_sb[:], u_sb[:], ALU.mult).then_inc(cu_ready, 1)

            def l1_body(h, last):
                n = h * L1_BODY + L1_PRE
                U = h * 4
                V = h * 5
                row_max(U + 2, 2)
                row_max(U + 3, 3)
                dve.wait_ge(cu_ready, h + 1)
                own.after(v.tensor_copy(cw_h[:].unsqueeze(1), cw[:, bass.ds(h, 1)]))
                own.after(v.tensor_scalar(z_a[:], cu[:, 0:T], cw_h[:, 0:1], None, ALU.mult))
                own.after(v.scalar_tensor_tensor(z_b[:], cu[:, 1:1 + T], cw_h[:, 1:2], z_a[:], ALU.mult, ALU.add))
                own.after(v.scalar_tensor_tensor(z_a[:], cu[:, 2:2 + T], cw_h[:, 2:3], z_b[:], ALU.mult, ALU.add))
                combine(U + 2, 2)
                combine(U + 3, 3)
                split_lo(n + 2, 1)
                t_out(V + 1, difT_hi[:, 0:3], difT_lo[:, 0:3])
                dve.wait_ge(bank_free, n + 3)
                own.after(v.tensor_tensor(z_b[:], z_a[:], b_sb[:], ALU.mult))
                own.after(v.tensor_copy(bzT_hi[:, bass.ds(h, 1)], z_b[:].unsqueeze(1)))
                v.tensor_tensor(bzT_lo[:, bass.ds(h, 1)], z_b[:].unsqueeze(1),
                                bzT_hi[:, bass.ds(h, 1)].bitcast(F32), ALU.subtract).then_inc(bz_ready, 1)
                split_lo(n + 3, 0)
                t_out(V + 2, difT_hi[:, TB:TB + 3], difT_lo[:, TB:TB + 3])
                if not last:
                    rope(n + 1, 0, h + 1)
                split_lo(n + 4, 1)
                t_out(V + 3, difT_hi[:, 0:TB], difT_lo[:, 0:TB])
                if not last:
                    rope(n + 2, 1, h + 1)
                split_lo(n + 5, 0)
                dve.wait_ge(o_squares, h * 4 + 5)
                rsqrt(P).then_inc(o_scale, 1)
                if not last:
                    first_scores(n + 4, U + 4, V + 4)
                v_on = V + (4 if last else 5)
                dve.wait_ge(t_hi, v_on + 1)
                v.scalar_tensor_tensor(attnT_lo[:, bass.ds(h, 1)], bank[:, 6].unsqueeze(1), subln_g[:, 0:1],
                                       attnT_hi[:, bass.ds(h, 1)].bitcast(F32), ALU.mult, ALU.subtract)\
                    .then_inc(t_lo, 1)

            split_lo(2, 0)
            rope(0, 0, 0)
            split_lo(3, 1)
            rope(1, 1, 0)
            split_lo(4, 0)
            first_scores(3, 0, 0)
            with own.repeat(H - 1, 33) as h:
                l1_body(h, False)
            l1_body(H - 1, True)

            def half_mixed(n):
                dve.wait_ge(bank_free, n + 3)
                v.tensor_tensor(m_a[:], sgc[:], yc_sb[:], ALU.mult).then_inc(half_mix, 1)

            def mix(i, n):
                dve.wait_ge(bank_free, n + 3)
                own.after(v.tensor_tensor(m_b[:], sga[:], ya_sb[:], ALU.mult))
                dve.wait_ge(half_mix, i + 1)
                own.after(v.tensor_tensor(m_c[:], m_a[:], m_b[:], ALU.add))
                own.after(v.tensor_copy(mixT_hi[:, bass.ds(i, 1)], m_c[:].unsqueeze(1)))
                v.tensor_tensor(mixT_lo[:, bass.ds(i, 1)], m_c[:].unsqueeze(1),
                                mixT_hi[:, bass.ds(i, 1)].bitcast(F32), ALU.subtract).then_inc(mix_done, 1)

            dve.wait_ge(t_lo, 5 * H + 1)
            half_mixed(N_L2 + 2)
            with own.repeat(DC - 1, 3) as i:
                n = i * 4 + (N_L2 + 3)
                split_lo(n + 2, 1)
                split_lo(n + 3, 0)
                mix(i, n + 1)
                split_lo(n + 4, 1)
                split_lo(n + 5, 0)
                half_mixed(n + 3)
            split_lo(N_WO + 1, 1)
            mix(DC - 1, N_WO - 1)
            for c in range(DC):
                split_lo(N_WO + c + 2, c)
            dve.wait_ge(w_used, N_PQ + 2)
            dve.wait_ge(x_in, 32)
            for b in range(TB):
                for q in range(2):
                    half = h_sb[:, b, q * 512:(q + 1) * 512]
                    v.tensor_tensor(half, bank[:, 2 * b + q], half, ALU.add).then_inc(h_ready, 1)
            norm(1, h_sb, xn_2)

            def q_out(s, c):
                dve.wait_ge(q_hi_done, s + 1)
                v.tensor_tensor(q_lo[:, c], bank[:, c], q_hi[:, c].bitcast(F32), ALU.subtract).then_inc(q_done, 1)

            q_out(0, 0)
            split_lo(N_PQ + 2, 0)
            with dve.Fori(0, PH - 1) as h:
                s = h * 2
                q_out(s + 1, 1)
                split_lo(s + (N_PQ + 3), 1)
                q_out(s + 2, 0)
                split_lo(s + (N_PQ + 4), 0)
            q_out(15, 1)
            split_lo(N_PQ + 17, 1)

            units = score[:].rearrange("p b h c n -> p (b h) c n")
            cand_flat = cand[:].rearrange("p a b -> p (a b)")
            val_out = sel[:, 2].rearrange("p b h k -> p (b h) k")
            key_out = sel[:, 0:2].rearrange("p c b h k -> p c (b h) k")

            def unit_step(i, j, halves, pairs, between=None):
                jobs = []
                if pairs:
                    jobs.append((cval, cidx, cand_flat, cand2[:]))
                if halves:
                    jobs += [(tval[:, c], tidx[:, c], sw[:, c], sw2[:, c]) for c in range(2)]
                if pairs:
                    v.tensor_copy(tidx_b[:], tidx[:])
                    v.tensor_tensor(cand[:], tval[:, 0].unsqueeze(2).to_broadcast([P, TOPK, TOPK]),
                                    tval[:, 1].unsqueeze(1).to_broadcast([P, TOPK, TOPK]), ALU.add)
                if halves:
                    v.tensor_copy(sw[:].unsqueeze(1), units[:, bass.ds(j, 1)])
                dve.drain()
                for val, idx, src, spare in jobs:
                    v.max(val[:, 0:8], src)
                dve.drain()
                for val, idx, src, spare in jobs:
                    v.match_replace(spare, val[:, 0:8], src, LOW)
                    v.max_index(idx[:, 0:8], val[:, 0:8], src)
                dve.drain()
                for val, idx, src, spare in jobs:
                    v.max(val[:, 8:16], spare)
                dve.drain()
                for val, idx, src, spare in jobs:
                    v.max_index(idx[:, 8:16], val[:, 8:16], spare)
                if between:
                    between()
                dve.drain()
                if not pairs:
                    return
                v.tensor_copy(val_out[:, bass.ds(i, 1)], cval[:].unsqueeze(1))
                v.tensor_single_scalar(crank[:, 0], cidx[:], 4, ALU.arith_shift_right)
                v.tensor_single_scalar(crank[:, 1], cidx[:], TOPK - 1, ALU.bitwise_and)
                dve.drain()
                v.tensor_copy(crank_b[:], crank[:].rearrange("p c k -> p (c k)").unsqueeze(2).to_broadcast([P, 2 * TOPK, 2]))
                dve.drain()
                shape = [P, 2 * TOPK, TOPK // 2, 2]
                v.tensor_tensor(pick[:].rearrange("p r (k j) -> p r k j", j=2),
                                crank_b[:].unsqueeze(2).to_broadcast(shape),
                                iota_b[:, 0:TOPK].rearrange("p (k j) -> p k j", j=2).unsqueeze(1).to_broadcast(shape),
                                ALU.is_equal)
                dve.drain()
                by_half = [t[:].rearrange("p (c r) k -> p c r k", c=2) for t in (pick, pick2)]
                v.tensor_tensor(by_half[1], by_half[0],
                                tidx_b[:].unsqueeze(2).to_broadcast([P, 2, TOPK, TOPK]), ALU.mult)
                dve.drain()
                for c in range(2):
                    v.tensor_reduce(key_out[:, c, bass.ds(i, 1)], by_half[1][:, c].unsqueeze(1), AX.X, ALU.add)

            dve.wait_ge(s_copied, 2 * PH + 2)
            v.tensor_copy(sw[:].unsqueeze(1), units[:, 0:1])
            dve.drain()
            unit_step(0, 0, True, False)
            with dve.Fori(0, 31) as i:
                c = i * 2
                unit_step(i, i + 1, True, True, lambda: split_lo(c + (N_A + 2), 0))
                split_lo(c + (N_A + 3), 1)
            unit_step(31, 0, False, True, lambda: split_lo(N_A + 64, 0))
            split_lo(N_A + 65, 1)
            dve.drain()

            top = sel[:, 2].rearrange("p b h k -> p (b h) k")
            best = gsum[:].unsqueeze(2)
            own.after(v.tensor_copy(best, top[:, :, 0:1]))
            v.tensor_tensor(top, top, best.to_broadcast([P, PH * TB, TOPK]), ALU.subtract).then_inc(top_shift, 1)
            dve.wait_ge(gate_exp, 1)
            own.after(v.tensor_reduce(gsum[:], top, AX.X, ALU.add))
            own.after(v.reciprocal(grec[:], gsum[:]))
            v.tensor_tensor(top, top, grec[:].unsqueeze(2).to_broadcast([P, PH * TB, TOPK]), ALU.mult)\
                .then_inc(sel_ready, 1)

            def bodies(t):
                return t.rearrange("p (b t) -> p b t", t=TOK)

            dve.wait_ge(selT_done, 1)
            v.tensor_copy(selT[:, :, 0], bodies(bank[:, 6])).then_inc(sel_used, 1)
            dve.wait_ge(selT_done, 2)
            v.tensor_copy(selT[:, :, 1], bodies(bank[:, 7])).then_inc(sel_used, 1)
            dve.wait_ge(selT_done, 3)
            v.tensor_copy(gateT[:], bank[:, 6]).then_inc(sel_used, 1)
            dve.wait_ge(sel_used, 3)
            own.after(v.tensor_copy(gpart[:], gateT[:]))
            own.after(v.tensor_copy(selT[:, :, 2], bodies(gpart[:])))
            own.after(v.tensor_tensor(grest[:], gateT[:], gpart[:], ALU.subtract))
            own.after(v.tensor_copy(gpart[:], grest[:]))
            own.after(v.tensor_copy(selT[:, :, 3], bodies(gpart[:])))
            own.after(v.tensor_tensor(selT[:, :, 4], bodies(grest[:]), bodies(gpart[:]), ALU.subtract))

            def spread_out(i, s):
                def keys4(t):
                    return t.rearrange("p t (k j) -> p t k j", j=4)

                def value(which):
                    row = which * TOK + s * 8
                    return tok5[:, row:row + 8].unsqueeze(2).to_broadcast([P, 8, NKEY // 4, 4])

                keys = iota_b[:].rearrange("p (k j) -> p k j", j=4).unsqueeze(1).to_broadcast([P, 8, NKEY // 4, 4])
                dve.wait_ge(g_full, i * 4 + (2 * s + 1))
                own.after(v.tensor_tensor(keys4(hit[:, s]), keys, value(0), ALU.is_equal))
                v.tensor_tensor(keys4(onehot[:, s, 0]), keys, value(1), ALU.is_equal)
                for q in range(3):
                    ins = v.tensor_tensor(keys4(onehot[:, s, 1 + q]), keys4(hit[:, s]), value(2 + q), ALU.mult)
                ins.then_inc(onehot_done, 1)

            def a2_body(i, last):
                c = i * 2 + 64
                dve.wait_ge(onehot_done, i * 2 + 1)
                own.after(v.tensor_copy(tok5[:].unsqueeze(1),
                                        selT[:, bass.ds(i, 1)].rearrange("p o a t -> p o (a t)").unsqueeze(3)
                                        .to_broadcast([P, 1, 5 * TOK, 4])))
                spread_out(i, 0)
                split_lo(c + (N_A + 2), 0)
                spread_out(i, 1)
                if not last:
                    split_lo(c + (N_A + 3), 1)

            with own.repeat(31, 3) as i:
                a2_body(i, False)
            a2_body(31, True)

            def product(c, k, slot, e, landed):
                dve.wait_ge(gb_in[slot], landed)
                dve.wait_ge(hb_in[k], (c - k) * 8 + 16)
                dve.wait_ge(act_lo_done, c + 1)
                v.tensor_tensor(prod[:, k].rearrange("p (b t) -> p b t", t=TOK),
                                h_buf[:, k].rearrange("p (b t) -> p b t", t=TOK),
                                g_buf[:, slot, :, e].rearrange("p b e t -> p b (e t)"), ALU.mult)\
                    .then_inc(prod_done, 1)
                dve.wait_ge(act_hi_done, c + 1)
                v.tensor_tensor(act_lo[:, k], prod[:, k], act_hi[:, k].bitcast(F32), ALU.subtract)\
                    .then_inc(act_lo_done, 1)

            def b_eight(o, slot, last=False):
                def two(r, split):
                    for k in range(2):
                        c = o * 16 + r * 2 + (8 * slot + k)
                        product(c, k, slot, bass.ds(r * 2 + k, 1), o * 32 + 32)
                        if split:
                            split_lo(c + (N_B + 1), k + 1)

                with dve.Fori(0, 3 if last else 4) as r:
                    two(r, True)
                if last:
                    product(126, 0, slot, bass.ds(6, 1), 256)
                    split_lo(N_B + 127, 1)
                    product(127, 1, slot, bass.ds(7, 1), 256)

            with dve.Fori(0, 7) as o:
                b_eight(o, 0)
                b_eight(o, 1)
            b_eight(7, 0)
            b_eight(7, 1, last=True)

            dve.wait_ge(y_done, 1)
            for b in range(TB):
                for q in range(2):
                    half = h_sb[:, b, q * 512:(q + 1) * 512]
                    v.tensor_tensor(half, bank[:, 2 * b + q], half, ALU.add).then_inc(y_sum, 1)
            dve.wait_ge(y_sq, TB)
            own.after(rsqrt(D))
            for b in range(TB):
                v.scalar_tensor_tensor(o_sb[:, b], h_sb[:, b], rs_y[:, b:b + 1], gfin[:], ALU.mult, ALU.mult)\
                    .then_inc(o_ready, 1)

        @block.tensor
        def _(pe):
            def three(dst, a_hi, a_lo, b_hi, b_lo, start, stop, **kw):
                pe.matmul(dst, a_hi, b_hi, start=start, stop=False, **kw)
                pe.matmul(dst, a_hi, b_lo, start=False, stop=False, **kw)
                return pe.matmul(dst, a_lo, b_hi, start=False, stop=stop, **kw)

            def norm(k, tile):
                pe.wait_ge(n_x[k], TB)
                for c in range(DC):
                    for b in range(TB):
                        last = pe.transpose(bank[:, c, b * P:(b + 1) * P], tile[:, b, c * P:(c + 1) * P], ident[:])
                    last.then_inc(n_t[k], 1)
                pe.wait_ge(n_lo[k], DC)

            pe.wait_ge(const_in, 16 * 4)
            norm(0, x_sb)

            def section(n, par, rhs_hi=xT_hi, rhs_lo=xT_lo, free=bank_free, freed=0):
                s = par % 2
                pe.wait_ge(w_lo_done, n + 3)
                pe.wait_ge(free, n + (1 - freed))
                a_hi, a_lo = w_tile(w_hi, s), w_tile(w_lo, s)
                for c in range(DC):
                    last = three(bank[:, s], a_hi[:, c], a_lo[:, c], rhs_hi[:, c], rhs_lo[:, c], c == 0, c == DC - 1)
                last.then_inc(w_used, 1)

            def scores(U, u):
                s, nk = u % 2, (u + 1) * P
                pe.wait_ge(exp_done, U + 1)
                for m in range(2):
                    rows = slice(m * HD, (m + 1) * HD)
                    scores_m = bank[:, 2 + 2 * s + m]
                    three(scores_m[:, 0:nk], qk_hi[rows, 0, u * P:nk], qk_lo[rows, 0, u * P:nk],
                          qk_hi[rows, 1, 0:nk], qk_lo[rows, 1, 0:nk], True, False)
                    last = pe.matmul(scores_m[:, u * P:nk], ident_b[:], mask_b[:], start=False, stop=True)
                last.then_inc(scores_done, 1)

            def t_wait(V):
                pe.wait_ge(t_lo, V + 1)

            def turn(U, V, units):
                pe.wait_ge(dif_ready, U + (units[-1] + 3))
                t_wait(V)
                first = P * (units[0] * (units[0] + 1) // 2)
                for c in range(sum(u + 1 for u in units)):
                    at = first + c * P
                    last = pe.transpose(bank[:, 6, c * P:(c + 1) * P], dif[:, at:at + P], ident[:])
                last.then_inc(t_full, 1)

            def attend(V, u, first):
                pe.wait_ge(t_lo, V + 2)
                for c in range(u + 1):
                    last = three(bank[:, 7, u * P:(u + 1) * P], difT_hi[:, first + c], difT_lo[:, first + c],
                                 v_hi[:, c], v_lo[:, c], c == 0, c == u)
                last.then_inc(pv_done, 1)

            def first_scores(n, U, V, h):
                section(n, 1)
                pe.wait_ge(bank_free, n + 2)
                t_wait(V)
                for b in range(TB):
                    ins = pe.transpose(bank[:, 6, b * P:(b + 1) * P], vT_sb[:, b * P:(b + 1) * P], ident[:])
                ins.then_inc(t_full, 1)
                pe.wait_ge(qk_ready, h * 2 + 3)
                scores(U, 0)
                scores(U + 1, 1)
                section(n + 1, 0)

            def l1_body(h, last):
                n = h * L1_BODY + L1_PRE
                U = h * 4
                V = h * 5
                scores(U + 2, 2)
                scores(U + 3, 3)
                section(n, 1)
                turn(U, V + 1, (0, 1))
                section(n + 1, 0)
                pe.wait_ge(on_ready, h + 1)
                attend(V + 1, 0, 0)
                attend(V + 1, 1, 1)
                turn(U, V + 2, (2,))
                section(n + 2, 1)
                attend(V + 2, 2, TB)
                turn(U, V + 3, (3,))
                if last:
                    pe.wait_ge(bz_ready, H + 1)
                    section(n + 3, 0, bzT_hi, bzT_lo)
                else:
                    section(n + 3, 0)
                attend(V + 3, 3, 0)
                if not last:
                    first_scores(n + 4, U + 4, V + 4, h + 1)
                else:
                    section(N_L2 + 3, 1)
                pe.wait_ge(on_ready, h + 2)
                t_wait(V + (4 if last else 5))
                for u in range(TB):
                    ins = pe.transpose(bank[:, 6, u * P:(u + 1) * P], on_sb[:, u], ident[:])
                ins.then_inc(t_full, 1)

            for n in range(3):
                section(n, n)
            pe.wait_ge(mask_ready, 2)
            first_scores(3, 0, 0, 0)
            with pe.Fori(0, H - 1) as h:
                l1_body(h, False)
            l1_body(H - 1, True)

            def ga_yc(n):
                section(n + 2, 1)
                section(n + 3, 0, bzT_hi, bzT_lo)

            pe.wait_ge(t_lo, 5 * H + 1)
            section(N_L2 + 4, 0, attnT_hi, attnT_lo)
            ga_yc(N_L2 + 3)
            with pe.Fori(0, DC - 2) as i:
                n = i * 4 + (N_L2 + 7)
                section(n, 1)
                section(n + 1, 0, attnT_hi, attnT_lo)
                ga_yc(n)
            section(N_WO - 1, 1, attnT_hi, attnT_lo)

            def add_rows(a_hi, a_lo, s, **kw):
                for b in range(TB):
                    for q in range(2):
                        cols = slice(q * 512, (q + 1) * 512)
                        last = three(bank[:, 2 * b + q], a_hi[:, b * P:(b + 1) * P], a_lo[:, b * P:(b + 1) * P],
                                     w_hi[:, s, cols], w_lo[:, s, cols], **kw)
                return last

            pe.wait_ge(mix_done, DC + 1)
            pe.wait_ge(bank_free, N_WO + 2)
            for c in range(DC):
                pe.wait_ge(w_lo_done, N_WO + c + 3)
                add_rows(mixT_hi[:, c], mixT_lo[:, c], c % 2, start=c == 0, stop=c == DC - 1).then_inc(w_used, 1)
            norm(1, xn_2)

            def key_scores(s, c):
                pe.wait_ge(q_done, s + 3)
                pe.wait_ge(key_lo, 1)
                pe.wait_ge(s_copied, s + 1)
                for b in range(TB):
                    toks = slice(b * P, (b + 1) * P)
                    last = three(bank[:, 2 + c, toks], q_hi[:, c, toks], q_lo[:, c, toks],
                                 keysT_hi[:, c], keysT_lo[:, c], True, True)
                last.then_inc(s_done, 1)

            def query(s, c):
                section(s + N_PQ, c, free=q_done, freed=N_PQ)

            query(0, 0)
            with pe.Fori(0, PH - 1) as h:
                s = h * 2
                query(s + 1, 1)
                key_scores(s, 0)
                query(s + 2, 0)
                key_scores(s + 1, 1)
            query(15, 1)
            key_scores(14, 0)
            key_scores(15, 1)
            pe.wait_ge(s_copied, 2 * PH + 2)

            def experts(c, k):
                pe.wait_ge(w_lo_done, c + (N_A + 3))
                pe.wait_ge(gel_done, c + 1)
                u_hi, u_lo = w_tile(w_hi, k), w_tile(w_lo, k)
                for q in range(DC):
                    last = three(bank[:, 4 + k], u_hi[:, q], u_lo[:, q], xT_hi[:, q], xT_lo[:, q],
                                 q == 0, q == DC - 1)
                last.then_inc(w_used, 1)

            def spread(i, j):
                if j % 2 == 0:
                    pe.wait_ge(onehot_done, i * 2 + (j // 2 + 2))
                pe.wait_ge(g_copied, i * 4 + (j + 1))
                for t in range(4):
                    own_t = j % 2 * 4 + t
                    for q in range(3):
                        last = pe.matmul(bank[:, 6 + j % 2, t * P:(t + 1) * P], onehot[:, j // 2, 0, own_t],
                                         onehot[:, j // 2, 1 + q, own_t], start=q == 0, stop=q == 2)
                last.then_inc(g_full, 1)

            with pe.Fori(0, 32) as i:
                experts(i * 2, 0)
                experts(i * 2 + 1, 1)
            pe.wait_ge(sel_ready, 1)
            for q in range(3):
                if q == 2:
                    pe.wait_ge(sel_used, 1)
                for b in range(TB):
                    last = pe.transpose(bank[:, 6 + q % 2, b * P:(b + 1) * P], sel[:, q, b].rearrange("p h k -> p (h k)"), ident[:])
                last.then_inc(selT_done, 1)
            pe.wait_ge(sel_used, 3)

            with pe.Fori(0, 32) as i:
                c = i * 2 + 64
                experts(c, 0)
                spread(i, 0)
                spread(i, 1)
                experts(c + 1, 1)
                spread(i, 2)
                spread(i, 3)

            pe.wait_ge(gel_done, NKEY + 2)
            pe.wait_ge(g_copied, T // 4 + 2)
            for q in range(8):
                pe.matmul(bank[:, q], zero_b[:, 0:P], zero_b[:], start=True, stop=False)
            with pe.Fori(0, NKEY // 2) as i:
                for k in range(2):
                    c = i * 2 + k
                    pe.wait_ge(act_lo_done, c + 3)
                    pe.wait_ge(w_lo_done, c + (N_B + 3))
                    add_rows(act_hi[:, k], act_lo[:, k], k, start=False, stop=False).then_inc(w_used, 1)
            for q in range(8):
                last = pe.matmul(bank[:, q], zero_b[:, 0:P], zero_b[:], start=False, stop=True)
            last.then_inc(y_done, 1)


def constants():
    import numpy as np
    f = np.float32
    inv = np.power(f(10000.0), -np.arange(0, HD, 2, dtype=f) / f(HD)).astype(f)
    ang = (np.arange(T, dtype=f)[None, :] * inv[:, None]).astype(f)
    cos, sin = np.cos(ang.astype(np.float64)).astype(f), np.sin(ang.astype(np.float64)).astype(f)
    row = np.arange(P)
    return {
        "c_cos": np.concatenate([cos] * 4),
        "c_sin": np.concatenate([-sin, sin] * 2),
        "c_ident": np.eye(P, dtype=f),
        "c_mask": np.where(row[None, :] <= row[:, None], f(0), f(-1e30)).astype(f),
        "c_iota": np.tile(row.astype(f), (P, 1)),
    }


def kernel(**inputs):
    import numpy as _np
    import concourse.bacc as _bacc
    from concourse import mybir as _mybir
    from concourse.bass_utils import run_bass_kernel_spmd as _run

    given = {name: _np.asarray(a) for name, a in inputs.items()}

    def tiles(w):
        return w.reshape(DC, P, -1, P).transpose(2, 1, 0, 3).reshape(-1, P, D)

    laid = {
        "x": given["x"],
        "norm_gains": _np.stack([given["norm1_g"][0], given["norm2_g"][0]]).reshape(2, DC, P).transpose(2, 0, 1),
        "w_in": tiles(given["w_in"][0]),
        "conv_w": given["conv_w"][0].reshape(KCONV, DC, P).transpose(2, 1, 0),
        "w_out_conv": tiles(given["w_out_conv"][0]),
        "lambdas": _np.stack([given[f"lambda_{n}"][0] for n in ("q1", "k1", "q2", "k2")]),
        "attn_subln_g": given["attn_subln_g"],
        "w_out_attn": tiles(given["w_out_attn"][0]),
        "w_o": given["w_o"],
        "peer_w_q": tiles(given["peer_w_q"][0]),
        "peer_keys": _np.stack([given["peer_keys1"][0].T, given["peer_keys2"][0].T], axis=1),
        "peer_u": tiles(given["peer_u"][0].T),
        "peer_v": given["peer_v"],
        "final_norm_g": given["final_norm_g"],
    }
    laid.update(constants())

    nc = _bacc.Bacc("TRN2", target_bir_lowering=False, num_devices=1)
    arrays, args = {}, []
    for name, value in laid.items():
        a = _np.ascontiguousarray(value)
        arrays[f"in_{name}"] = a
        args.append(nc.dram_tensor(f"in_{name}", a.shape, _mybir.dt.from_np(a.dtype), kind="ExternalInput").ap())
    args.append(nc.dram_tensor("out_0", (1, T, D), _mybir.dt.float32, kind="ExternalOutput").ap())
    peer_block(nc, *args)
    r = _run(nc, [arrays], core_ids=[0])
    return r.results[0]["out_0"]
```

```python
from contextlib import ExitStack, contextmanager

import concourse.bass as bass
from concourse import mybir

F32 = mybir.dt.float32
F32R = mybir.dt.float32r
BF16 = mybir.dt.bfloat16
I32 = mybir.dt.int32
U32 = mybir.dt.uint32
ACT = mybir.ActivationFunctionType
ALU = mybir.AluOpType
AX = mybir.AxisListType

P = 128
D = 1024
T = 512
DC = D // P
TB = T // P
H = 8
HD = D // (2 * H)
KCONV = 3
PH = 8
TOPK = 16
NKEY = 128
LAM_INIT = 0.8 - 0.6
SCALE = HD ** -0.5
EPS = 1e-6
LOW = -3.0e38
RSQRT_MAGIC = 0x5F3759DF

L1_PRE = 5
L1_BODY = 6
N_L2 = L1_BODY * H
N_WO = N_L2 + 4 * DC
N_PQ = N_WO + DC
N_A = N_PQ + 2 * PH
N_B = N_A + NKEY
N_END = N_B + NKEY
SECTION = {"b": 0, "c": 1, "u": 2, "q": 3, "k": 4, "v": 5, "gc": 6, "ga": 7}
TOK = 16
BODIES = T // TOK


class Steps:

    def __init__(self, eng, sem):
        self.eng, self.sem, self.base, self.k, self.loops = eng, sem, 0, 0, []

    def value(self):
        v = self.base + self.k
        for i, per in self.loops:
            v = i * per + v
        return v

    def after(self, ins):
        self.end(ins)
        self.wait()

    def end(self, ins):
        ins.then_inc(self.sem, 1)
        self.k += 1

    def wait(self):
        self.eng.wait_ge(self.sem, self.value())

    @contextmanager
    def repeat(self, count, per):
        base, k = self.base, self.k
        with self.eng.Fori(0, count) as i:
            self.base, self.k = base + k, 0
            self.loops.append((i, per))
            yield i
            assert self.k == per, (self.k, per)
            self.loops.pop()
        self.base, self.k = base + k + count * per, 0


def peer_block(nc, x, norm_gains, w_in, conv_w, w_out_conv, lambdas, attn_subln_g, w_out_attn, w_o, peer_w_q,
               peer_keys, peer_u, peer_v, final_norm_g, c_cos, c_sin, c_ident, c_mask, c_iota, out):
    gel_dram = nc.dram_tensor("gelu_spill", (NKEY, P, T), F32, kind="Internal").ap()
    gate_dram = nc.dram_tensor("gate_spill", (BODIES, P, NKEY + 4, TOK), F32, kind="Internal").ap()

    wo_v = w_o[0].rearrange("(c p) n -> c p n", p=P)
    v_v = peer_v[0].rearrange("(c p) d -> c p d", p=P)
    x_v = x[0].rearrange("(b p) d -> p b d", p=P)
    out_v = out[0].rearrange("(b p) d -> b p d", p=P)

    ctx = ExitStack()
    with ctx:
        def sem(name):
            return ctx.enter_context(nc.semaphore(name))

        def space(stack):
            return lambda name, shape, dt=F32: stack.enter_context(nc.sbuf_tensor(name, shape, dt))

        sb = space(ctx)
        ident = sb("ident", [P, P])
        iota_f = sb("iota_f", [P, P])
        iota_b = sb("iota_b", [P, P], BF16)
        zero_b = sb("zero_b", [P, T], BF16)
        norm_g = sb("norm_g", [P, 2, DC])
        gfin = sb("gfin", [P, D])
        xT_hi = sb("xT_hi", [P, DC, T], F32R)
        xT_lo = sb("xT_lo", [P, DC, T], F32R)
        w_raw = sb("w_raw", [P, 2, D])
        w_hi = sb("w_hi", [P, 2, D], F32R)
        w_lo = sb("w_lo", [P, 2, D], F32R)
        keysT_hi = sb("keysT_hi", [P, 2, NKEY], F32R)
        keysT_lo = sb("keysT_lo", [P, 2, NKEY], F32R)
        stat = sb("stat", [P, 4])
        rs_a = sb("rs_a", [P, 4])
        rs_i = sb("rs_i", [P, 4], I32)
        rs_t = sb("rs_t", [P, 4])
        rs_y = sb("rs_y", [P, 4])
        junk = sb("junk", [P, D])

        s0 = ExitStack()
        a = space(s0)
        x_sb = a("x_sb", [P, TB, D])
        keys_sb = a("keys_sb", [P, 2, NKEY])
        s0.close()
        sL = ExitStack()
        a = space(sL)
        attnT_hi = a("attnT_hi", [P, H, T], F32R)
        attnT_lo = a("attnT_lo", [P, H, T], F32R)
        bzT_hi = a("bzT_hi", [P, DC, T], F32R)
        bzT_lo = a("bzT_lo", [P, DC, T], F32R)
        sgc = a("sgc", [P, T])
        sga = a("sga", [P, T])
        yc_sb = a("yc_sb", [P, T])
        s1 = ExitStack()
        a = space(s1)
        cos_t = a("cos_t", [P, T])
        sin_t = a("sin_t", [P, T])
        mask_t = a("mask_t", [P, P])
        mask_b = a("mask_b", [P, P], BF16)
        ident_b = a("ident_b", [P, P], BF16)
        cw = a("cw", [P, DC, KCONV])
        cw_h = a("cw_h", [P, KCONV])
        subln_g = a("subln_g", [P, 1])
        lam4 = a("lam4", [P, 4, HD])
        lam_p = a("lam_p", [P, 2, HD])
        lam_s = a("lam_s", [P, 2])
        neg_lam = a("neg_lam", [P, 1])
        qk_raw = a("qk_raw", [P, 2, T])
        qk_rot = a("qk_rot", [P, 2, T])
        rope_a = a("rope_a", [P, T])
        rope_b = a("rope_b", [P, T])
        qk_hi = a("qk_hi", [P, 2, T], F32R)
        qk_lo = a("qk_lo", [P, 2, T], F32R)
        vT_sb = a("vT_sb", [P, T])
        v_hi = a("v_hi", [P, TB, P], F32R)
        v_lo = a("v_lo", [P, TB, P], F32R)
        c_sb = a("c_sb", [P, T])
        u_sb = a("u_sb", [P, T])
        b_sb = a("b_sb", [P, T])
        cu = a("cu", [P, T + KCONV - 1])
        z_a = a("z_a", [P, T])
        z_b = a("z_b", [P, T])
        nbias = a("nbias", [P, 2, 2])
        prob = a("prob", [P, 2, 2, T])
        zsum = a("zsum", [P, 2, 2])
        rz = a("rz", [P, 2, 2])
        p1s = a("p1s", [P, T])
        dif = a("dif", [P, P * (1 + 2 + 3 + 4)])
        difT_hi = a("difT_hi", [P, TB + 3, P], F32R)
        difT_lo = a("difT_lo", [P, TB + 3, P], F32R)
        on_sb = a("on_sb", [P, TB, P])
        s1.close()
        s2 = ExitStack()
        a = space(s2)
        mixT_hi = a("mixT_hi", [P, DC, T], F32R)
        mixT_lo = a("mixT_lo", [P, DC, T], F32R)
        ya_sb = a("ya_sb", [P, T])
        m_a = a("m_a", [P, T])
        m_b = a("m_b", [P, T])
        m_c = a("m_c", [P, T])
        s2.close()
        sL.close()
        h_sb = sb("h_sb", [P, TB, D])
        sN = ExitStack()
        xn_2 = space(sN)("xn_2", [P, TB, D])
        sN.close()
        sP = ExitStack()
        a = space(sP)
        score = a("score", [P, TB, PH, 2, NKEY])
        q_hi = a("q_hi", [P, 2, T], F32R)
        q_lo = a("q_lo", [P, 2, T], F32R)
        sw = a("sw", [P, 2, NKEY])
        sw2 = a("sw2", [P, 2, NKEY])
        tval = a("tval", [P, 2, TOPK])
        tidx = a("tidx", [P, 2, TOPK], U32)
        tidx_b = a("tidx_b", [P, 2, TOPK], BF16)
        cand = a("cand", [P, TOPK, TOPK])
        cand2 = a("cand2", [P, TOPK * TOPK])
        cval = a("cval", [P, TOPK])
        cidx = a("cidx", [P, TOPK], U32)
        crank = a("crank", [P, 2, TOPK], U32)
        crank_b = a("crank_b", [P, 2 * TOPK, 2], BF16)
        pick = a("pick", [P, 2 * TOPK, TOPK], BF16)
        pick2 = a("pick2", [P, 2 * TOPK, TOPK], BF16)
        sel = a("sel", [P, 3, TB, PH, TOPK])
        gsum = a("gsum", [P, PH * TB])
        grec = a("grec", [P, PH * TB])
        selT = a("selT", [P, BODIES, 5, TOK], BF16)
        grest = a("grest", [P, T])
        tok5 = a("tok5", [P, 5 * TOK, 4], BF16)
        hit = a("hit", [P, 2, 8, NKEY], BF16)
        onehot = a("onehot", [P, 2, 4, 8, NKEY], BF16)
        g_stage = a("g_stage", [P, NKEY, TOK])
        g_stage_end = a("g_stage_end", [P, NKEY, TOK])
        gel = a("gel", [P, 2, T])
        sP.close()
        sB = ExitStack()
        a = space(sB)
        g_buf = a("g_buf", [P, 2, BODIES, 8, TOK])
        h_buf = a("h_buf", [P, 2, T])
        prod = a("prod", [P, 2, T])
        act_hi = a("act_hi", [P, 2, T], F32R)
        act_lo = a("act_lo", [P, 2, T], F32R)
        o_sb = a("o_sb", [P, TB, D])
        sB.close()

        bank = ctx.enter_context(nc.psum_tensor("bank", [P, 8, 512], F32))

        const_in = sem("const_in")
        ident_in = sem("ident_in")
        x_in = [sem(f"x_landed{b}") for b in range(TB)]
        x_again = sem("x_again")
        key_in = sem("key_in")
        consts_out = sem("consts_out")
        key_hi = sem("key_hi")
        key_lo = sem("key_lo")
        lam_exp = sem("lam_exp")
        lam_dot = sem("lam_dot")
        w_in_sem = [sem("w_landed0"), sem("w_landed1")]
        w_hi_done = sem("w_hi_done")
        w_lo_done = sem("w_lo_done")
        w_used = sem("w_used")
        bank_free = sem("bank_free")
        dve_own = sem("dve_own")
        n_sq = [sem(f"n{k}_squares") for k in (1, 2)]
        n_rs = [sem(f"n{k}_rsqrt") for k in (1, 2)]
        n_x = [sem(f"n{k}_scaled") for k in (1, 2)]
        n_t = [sem(f"n{k}_transposed") for k in (1, 2)]
        n_hi = [sem(f"n{k}_hi") for k in (1, 2)]
        n_lo = [sem(f"n{k}_lo") for k in (1, 2)]
        mask_ready = sem("mask_ready")
        qk_ready = sem("qk_ready")
        cu_ready = sem("cu_ready")
        bz_ready = sem("bz_ready")
        scores_done = sem("scores_done")
        bias_ready = sem("bias_ready")
        exp_done = sem("exp_done")
        dif_ready = sem("dif_ready")
        t_full = sem("t_full")
        t_hi = sem("t_hi")
        t_lo = sem("t_lo")
        pv_done = sem("pv_done")
        o_squares = sem("o_squares")
        o_scale = sem("o_scale")
        on_ready = sem("on_ready")
        half_mix = sem("half_mix")
        mix_done = sem("mix_done")
        wo_done = sem("wo_done")
        h_ready = sem("h_ready")
        q_hi_done = sem("q_hi_done")
        q_done = sem("q_done")
        s_done = sem("s_done")
        s_copied = sem("s_copied")
        gel_done = sem("gel_done")
        gel_out = [sem("gel_stored0"), sem("gel_stored1")]
        top_shift = sem("top_shift")
        gate_exp = sem("gate_exp")
        keys_ready = sem("keys_ready")
        sel_ready = sem("sel_ready")
        sel_used = sem("sel_used")
        selT_done = sem("selT_done")
        onehot_done = [sem("onehot_done0"), sem("onehot_done1")]
        g_full = sem("g_full")
        g_copied = sem("g_copied")
        g_out = sem("g_stored")
        g_last = sem("g_last")
        gb_in = [sem("gates_landed0"), sem("gates_landed1")]
        hb_in = [sem("gelu_landed0"), sem("gelu_landed1")]
        prod_done = sem("prod_done")
        act_hi_done = sem("act_hi_done")
        act_lo_done = sem("act_lo_done")
        y_done = sem("y_done")
        y_sum = sem("y_sum")
        y_sq = sem("y_squares")
        y_rs = sem("y_rsqrt")
        o_ready = sem("o_ready")
        o_ready_last = sem("o_ready_last")
        stored = sem("stored")

        block = ctx.enter_context(nc.Block())

        def w_tile(t, n):
            return t[:, n % 2, :].rearrange("p (c n) -> p c n", c=DC)

        @block.sync
        def _(sp):
            for b in range(TB):
                sp.dma_start(x_sb[:, b], x_v[:, b]).then_inc(x_in[b], 16)
            sp.dma_start(ident[:], c_ident).then_inc(ident_in, 16)
            sp.dma_start(norm_g[:], norm_gains).then_inc(ident_in, 16)

            def load(n, par, src):
                sp.wait_ge(w_lo_done, n + 1)
                s = par % 2
                sp.dma_start(w_raw[:, s, :], src).then_inc(w_in_sem[s], 16)

            def section(name, h):
                return w_in[bass.ds(h + SECTION[name] * DC, 1)]

            for n, name in enumerate("qk"):
                load(n, n, section(name, 0))
            sp.dma_start(cos_t[:], c_cos).then_inc(consts_out, 16)
            sp.dma_start(sin_t[:], c_sin).then_inc(consts_out, 16)
            sp.dma_start(mask_t[:], c_mask).then_inc(consts_out, 16)
            sp.dma_start(cw[:], conv_w).then_inc(consts_out, 16)
            sp.dma_start(subln_g[:], attn_subln_g[0].rearrange("(p a) -> p a", a=1)).then_inc(consts_out, 16)
            sp.dma_start(lam4[:], lambdas.partition_broadcast(P)).then_inc(consts_out, 16)
            load(2, 0, section("v", 0))
            sp.dma_start(iota_f[:], c_iota).then_inc(const_in, 16)
            sp.dma_start(gfin[:], final_norm_g.partition_broadcast(P)).then_inc(const_in, 16)
            sp.dma_start(keys_sb[:], peer_keys).then_inc(key_in, 16)
            load(3, 1, section("c", 0))
            load(4, 0, section("u", 0))
            with sp.Fori(0, H - 1) as h:
                n = h * L1_BODY + L1_PRE
                load(n, 1, section("b", h))
                for j, name in enumerate("qkvcu"):
                    load(n + (1 + j), j, section(name, h + 1))
            load(N_L2 - 1, 1, section("b", H - 1))
            load(N_L2, 0, section("gc", 0))
            load(N_L2 + 1, 1, section("ga", 0))
            load(N_L2 + 2, 0, w_out_conv[0])
            with sp.Fori(0, DC - 1) as i:
                n = i * 4 + (N_L2 + 3)
                load(n, 1, section("gc", i + 1))
                load(n + 1, 0, w_out_attn[bass.ds(i, 1)])
                load(n + 2, 1, section("ga", i + 1))
                load(n + 3, 0, w_out_conv[bass.ds(i + 1, 1)])
            load(N_WO - 1, 1, w_out_attn[DC - 1])
            for c in range(DC):
                load(N_WO + c, N_WO + c, wo_v[c])
                if c == 1:
                    sp.wait_ge(w_used, N_WO + 2)
                    sp.dma_start(h_sb[:], x_v).then_inc(x_again, 16)
            with sp.Fori(0, PH) as h:
                for c in range(2):
                    load(h * 2 + (N_PQ + c), N_PQ + c, peer_w_q[bass.ds(h * 2 + c, 1)])

            for c in range(2):
                load(N_A + c, N_A + c, peer_u[c])

            def a_chunk(c, k, src):
                load(c + (N_A + 2), k, src)
                sp.wait_ge(gel_done, c + 3)
                sp.dma_start(gel_dram[bass.ds(c, 1)], gel[:, k]).then_inc(gel_out[k], 16)

            def a2_store(i, stage=g_stage):
                sp.wait_ge(g_copied, i * 4 + 6)
                sp.dma_start(gate_dram[bass.ds(i, 1), :, 0:NKEY], stage[:]).then_inc(g_out, 16)

            with sp.Fori(0, 32) as i:
                for k in range(2):
                    a_chunk(i * 2 + k, k, peer_u[bass.ds(i * 2 + (2 + k), 1)])
            a_chunk(64, 0, peer_u[66])
            with sp.Fori(0, 30) as i:
                a_chunk(i * 2 + 65, 1, peer_u[bass.ds(i * 2 + 67, 1)])
                a_chunk(i * 2 + 66, 0, peer_u[bass.ds(i * 2 + 68, 1)])
                a2_store(i)
            def gates_of(block_of_8, s, first, end):
                src = gate_dram[:, :, bass.ds(block_of_8 * 8, 8), :].rearrange("b p e t -> p b e t")
                sp.dma_start(g_buf[:, s, first:end], src[:, first:end]).then_inc(gb_in[s], 16)

            def gates(block_of_8, s):
                gates_of(block_of_8, s, 0, BODIES // 2)
                gates_of(block_of_8, s, BODIES // 2, BODIES)

            def gelus(c, k):
                sp.dma_start(h_buf[:, k], gel_dram[bass.ds(c, 1)]).then_inc(hb_in[k], 16)

            sp.wait_ge(g_out, 16 * (BODIES - 3))
            gates_of(0, 0, 0, BODIES // 2)
            a_chunk(125, 1, peer_u[127])
            sp.wait_ge(g_out, 16 * (BODIES - 1))
            gates_of(0, 0, BODIES // 2, BODIES - 2)
            a_chunk(126, 0, v_v[0])
            a2_store(30)
            sp.wait_ge(gel_out[0], 16 * 65)
            sp.wait_ge(gel_out[1], 16 * 64)
            gelus(0, 0)
            gelus(1, 1)
            a_chunk(127, 1, v_v[1])
            a2_store(31, g_stage_end)
            sp.wait_ge(gel_out[1], 16 * 65)

            def b_chunks(c, last=False):
                for k in range(2):
                    load(c + (N_B + 2 + k), k, v_v[bass.ds(c + (2 + k), 1)])
                    sp.wait_ge(prod_done, c + (3 + k))
                    gelus(c + (2 + k), k)

            def b_eight(o, s, first=0):
                with sp.Fori(first, 4) as r:
                    b_chunks(o * 16 + r * 2 + 8 * s)
                sp.wait_ge(prod_done, o * 16 + (8 * s + 10))
                gates(o * 2 + (2 + s), s)

            b_chunks(0)
            sp.wait_ge(g_out, 16 * (BODIES + 1))
            gates(1, 1)
            b_eight(0, 0, first=1)
            b_eight(0, 1)
            with sp.Fori(1, 7) as o:
                b_eight(o, 0)
                b_eight(o, 1)
            with sp.Fori(0, 7) as r:
                b_chunks(r * 2 + 112)
            for k, b in enumerate((TB - 1, *range(TB - 1))):
                if k:
                    sp.wait_ge(o_ready, k)
                else:
                    sp.wait_ge(o_ready_last, 1)
                sp.dma_start(out_v[b], o_sb[:, b]).then_inc(stored, 16)
            sp.wait_ge(stored, 16 * TB)

        @block.gpsimd
        def _(pool):
            for s, n in ((w_lo_done, 2), (w_used, 2), (bank_free, 2), (bz_ready, 1),
                         (exp_done, 2), (dif_ready, 2), (t_lo, 1), (pv_done, 2), (on_ready, 1), (o_squares, 1), (qk_ready, 1),
                         (mix_done, 1), (q_done, 2), (s_done, 2), (s_copied, 2), (gel_done, 2), (gel_out[0], 16), (gel_out[1], 16),
                         (g_full, 3), (g_copied, 2), (g_out, 16), (prod_done, 2), (act_lo_done, 2)):
                pool.sem_inc(s, n)

        @block.scalar
        def _(act):
            def copy(dst, src, **kw):
                return act.activation(dst, src, ACT.Copy, **kw)

            def split_hi(n, par):
                s = par % 2
                act.wait_ge(w_in_sem[s], (n - s) * 8 + 16)
                act.wait_ge(w_used, n + 1)
                copy(w_hi[:, s, :], w_raw[:, s, :]).then_inc(w_hi_done, 1)

            def norm(k, src, tile, ready, tiles):
                for b in range(TB):
                    ready(b)
                    if b:
                        act.wait_ge(n_sq[k], b)
                    act.activation(junk[:], src[:, b], ACT.Square, accum_out=stat[:, b:b + 1]).then_inc(n_sq[k], 1)
                for n in tiles:
                    split_hi(n, n)
                act.wait_ge(n_rs[k], 1)
                for b in range(1, TB, 2):
                    copy(tile[:, b], src[:, b], scale=rs_y[:, b:b + 1]).then_inc(n_x[k], 1)
                for c in range(DC):
                    act.wait_ge(n_t[k], c + 1)
                    copy(xT_hi[:, c], bank[:, c], scale=norm_g[:, k, c:c + 1]).then_inc(n_hi[k], 1)

            norm(0, x_sb, x_sb, lambda b: act.wait_ge(x_in[b], 16), (0, 1))
            act.wait_ge(lam_dot, 2)
            act.activation(lam_s[:], lam_s[:], ACT.Exp).then_inc(lam_exp, 1)

            def evac(n, par):
                act.wait_ge(w_used, n + 3)
                return bank[:, par % 2]

            def out_qk(n, par, which, h, first=False):
                src = evac(n, par)
                if not first:
                    act.wait_ge(qk_ready, h * 2 + which)
                scale = 1.0 if which else SCALE
                copy(qk_raw[:, which], src, scale=scale)
                for q in range(4):
                    d = q ^ 1
                    last = copy(qk_rot[32 * d:32 * d + 32, which], src[32 * q:32 * q + 32], scale=scale)
                last.then_inc(bank_free, 1)

            def t_out(v, dst, scale=None):
                act.wait_ge(t_full, v + 1)
                n = dst.shape[1]
                src = bank[:, 6, 0:n * P].rearrange("p (c n) -> p c n", c=n)
                kw = {} if scale is None else {"scale": scale}
                copy(dst, src, **kw).then_inc(t_hi, 1)

            def exps(U, u):
                sp_, nk = u % 2, (u + 1) * P
                act.wait_ge(bias_ready, U + 1)
                act.wait_ge(dif_ready, U + 1)
                for m in range(2):
                    ins = act.activation(prob[:, sp_, m, 0:nk], bank[:, 2 + 2 * sp_ + m, 0:nk], ACT.Exp,
                                         bias=nbias[:, sp_, m:m + 1],
                                         accum_out=zsum[:, sp_, m:m + 1])
                ins.then_inc(exp_done, 1)

            def squares(U, u):
                act.wait_ge(o_squares, U + 1)
                act.activation(junk[:, 0:P], bank[:, 7, u * P:(u + 1) * P], ACT.Square,
                               accum_out=stat[:, u:u + 1]).then_inc(o_squares, 1)

            def first_scores(n, U, V, h=None):
                if h is not None:
                    act.wait_ge(cu_ready, h + 1)
                copy(c_sb[:], evac(n, 1)).then_inc(bank_free, 1)
                split_hi(n + 2, 1)
                t_out(V, v_hi[:])
                exps(U, 0)
                exps(U + 1, 1)
                copy(u_sb[:], evac(n + 1, 0)).then_inc(bank_free, 1)
                split_hi(n + 3, 0)

            def l1_body(h, last):
                n = h * L1_BODY + L1_PRE
                U = h * 4
                V = h * 5
                exps(U + 2, 2)
                exps(U + 3, 3)
                act.wait_ge(bz_ready, h + 1)
                copy(b_sb[:], evac(n, 1)).then_inc(bank_free, 1)
                split_hi(n + 2, 1)
                act.wait_ge(pv_done, U + 2)
                t_out(V + 1, difT_hi[:, 0:3])
                if last:
                    act.activation(sgc[:], evac(n + 1, 0), ACT.Sigmoid).then_inc(bank_free, 1)
                else:
                    out_qk(n + 1, 0, 0, h + 1)
                split_hi(n + 3, 0)
                act.wait_ge(pv_done, U + 1)
                t_out(V + 2, difT_hi[:, TB:TB + 3])
                if last:
                    act.activation(sga[:], evac(n + 2, 1), ACT.Sigmoid).then_inc(bank_free, 1)
                else:
                    out_qk(n + 2, 1, 1, h + 1)
                split_hi(n + 4, 1)
                act.wait_ge(pv_done, U + 4)
                t_out(V + 3, difT_hi[:, 0:TB])
                copy(yc_sb[:] if last else vT_sb[:], evac(n + 3, 0)).then_inc(bank_free, 1)
                split_hi(n + 5, 0)
                act.wait_ge(pv_done, U + TB + 2)
                for u in range(TB):
                    squares(U + u, u)
                act.wait_ge(o_scale, h + 1)
                for u in range(TB):
                    ins = copy(on_sb[:, u], bank[:, 7, u * P:(u + 1) * P], scale=rs_y[:, u:u + 1])
                ins.then_inc(on_ready, 1)
                if not last:
                    first_scores(n + 4, U + 4, V + 4, h)
                v_on = V + (4 if last else 5)
                act.wait_ge(t_full, v_on + 1)
                copy(attnT_hi[:, bass.ds(h, 1)], bank[:, 6].unsqueeze(1), scale=subln_g[:, 0:1]).then_inc(t_hi, 1)

            act.wait_ge(consts_out, 16 * 6)
            out_qk(0, 0, 0, 0, first=True)
            split_hi(2, 0)
            out_qk(1, 1, 1, 0, first=True)
            split_hi(3, 1)
            copy(vT_sb[:], evac(2, 0)).then_inc(bank_free, 1)
            split_hi(4, 0)
            act.wait_ge(key_in, 16)
            copy(keysT_hi[:], keys_sb[:]).then_inc(key_hi, 1)
            first_scores(3, 0, 0)
            with act.Fori(0, H - 1) as h:
                l1_body(h, False)
            l1_body(H - 1, True)

            with act.Fori(0, DC - 1) as i:
                n = i * 4 + (N_L2 + 3)
                act.wait_ge(half_mix, i + 1)
                act.activation(sgc[:], evac(n, 1), ACT.Sigmoid).then_inc(bank_free, 1)
                split_hi(n + 2, 1)
                act.wait_ge(mix_done, i + 1)
                copy(ya_sb[:], evac(n + 1, 0)).then_inc(bank_free, 1)
                split_hi(n + 3, 0)
                act.wait_ge(mix_done, i + 2)
                act.activation(sga[:], evac(n + 2, 1), ACT.Sigmoid).then_inc(bank_free, 1)
                split_hi(n + 4, 1)
                copy(yc_sb[:], evac(n + 3, 0)).then_inc(bank_free, 1)
                split_hi(n + 5, 0)
            act.wait_ge(mix_done, DC)
            copy(ya_sb[:], evac(N_WO - 1, 1)).then_inc(bank_free, 1)
            split_hi(N_WO + 1, 1)
            for c in range(DC - 1):
                split_hi(N_WO + c + 2, c)
            norm(1, h_sb, xn_2, lambda b: act.wait_ge(h_ready, 2 * b + 2), (N_PQ + 1,))

            def q_out(s, c):
                act.wait_ge(w_used, s + (N_PQ + 3))
                act.wait_ge(s_done, s + 1)
                copy(q_hi[:, c], bank[:, c]).then_inc(q_hi_done, 1)

            def s_out(h, s, c):
                act.wait_ge(s_done, s + 3)
                copy(score[:, :, bass.ds(h, 1), c],
                     bank[:, 2 + c].rearrange("p (b a n) -> p b a n", a=1, b=TB)).then_inc(s_copied, 1)

            q_out(0, 0)
            split_hi(N_PQ + 2, 0)
            with act.Fori(0, PH - 1) as h:
                s = h * 2
                q_out(s + 1, 1)
                split_hi(s + (N_PQ + 3), 1)
                s_out(h, s, 0)
                q_out(s + 2, 0)
                split_hi(s + (N_PQ + 4), 0)
                s_out(h, s + 1, 1)
            q_out(15, 1)
            split_hi(N_PQ + 17, 1)
            s_out(PH - 1, 14, 0)
            s_out(PH - 1, 15, 1)

            def gelu(c, k, split=True):
                act.wait_ge(w_used, c + (N_A + 3))
                act.wait_ge(gel_out[k], (c - k) * 8 + 16)
                act.activation(gel[:, k], bank[:, 4 + k], ACT.Gelu).then_inc(gel_done, 1)
                if split:
                    split_hi(c + (N_A + 2), k)

            def g_group(g, slot, k, stage):
                act.wait_ge(g_full, g + 4)
                copy(stage[:, :, 4 * k:4 * k + 4], bank[:, 6 + slot].rearrange("p (t e) -> p e t", t=4))\
                    .then_inc(g_copied, 1)

            with act.Fori(0, 32) as i:
                gelu(i * 2, 0)
                gelu(i * 2 + 1, 1)
            act.wait_ge(top_shift, 1)
            act.activation(sel[:, 2], sel[:, 2], ACT.Exp).then_inc(gate_exp, 1)
            for q in range(2):
                act.wait_ge(selT_done, q + 1)
                copy(selT[:, :, q], bank[:, 6 + q].rearrange("p (b t) -> p b t", t=TOK)).then_inc(sel_used, 1)
            gelu(64, 0)

            def g_groups(i, first, stage=g_stage):
                if first == 0 and stage is g_stage:
                    act.wait_ge(g_out, i * 16 + 16)
                for j in (first, first + 1):
                    g_group(i * 4 + j, j % 2, j, stage)

            with act.Fori(0, 31) as i:
                gelu(i * 2 + 65, 1)
                g_groups(i, 0)
                gelu(i * 2 + 66, 0)
                g_groups(i, 2)
            gelu(127, 1, split=False)
            g_groups(31, 0, g_stage_end)
            g_groups(31, 2, g_stage_end)

            def b_chunk(c, k, split=True):
                act.wait_ge(prod_done, c + 3)
                act.wait_ge(w_used, c + (N_B + 1))
                copy(act_hi[:, k], prod[:, k]).then_inc(act_hi_done, 1)
                if split:
                    split_hi(c + (N_B + 1), k + 1)

            with act.Fori(0, 63) as i:
                for k in range(2):
                    b_chunk(i * 2 + k, k)
            b_chunk(126, 0)
            b_chunk(127, 1, split=False)
            for b in range(TB):
                act.wait_ge(y_sum, 2 * b + 2)
                if b:
                    act.wait_ge(y_sq, b)
                act.activation(junk[:], h_sb[:, b], ACT.Square, accum_out=stat[:, b:b + 1]).then_inc(y_sq, 1)
            act.wait_ge(y_rs, 1)
            copy(o_sb[:, TB - 1], o_sb[:, TB - 1], scale=rs_y[:, TB - 1:TB]).then_inc(o_ready_last, 1)

        @block.vector
        def _(dve):
            v = nc.vector
            own = Steps(dve, dve_own)

            def split_lo(n, par):
                s = par % 2
                dve.wait_ge(w_hi_done, n + 1)
                v.tensor_tensor(w_lo[:, s, :], w_raw[:, s, :], w_hi[:, s, :].bitcast(F32), ALU.subtract)\
                    .then_inc(w_lo_done, 1)

            def rsqrt(width):
                own.after(v.tensor_scalar(rs_a[:], stat[:], 1.0 / width, EPS, ALU.mult, ALU.add))
                own.after(v.tensor_single_scalar(rs_i[:], rs_a[:].bitcast(I32), 1, ALU.arith_shift_right))
                own.after(v.tensor_scalar(rs_y[:].bitcast(I32), rs_i[:], -1.0, float(RSQRT_MAGIC), ALU.mult, ALU.add))
                for k in range(3):
                    own.after(v.scalar_tensor_tensor(rs_t[:], rs_y[:], -0.5, rs_y[:], ALU.mult, ALU.mult))
                    own.after(v.tensor_tensor(rs_t[:], rs_t[:], rs_a[:], ALU.mult))
                    ins = v.scalar_tensor_tensor(rs_y[:], rs_t[:], 1.5, rs_y[:], ALU.add, ALU.mult)
                    if k < 2:
                        own.after(ins)
                return ins

            def norm(k, src, tile, tiles):
                dve.wait_ge(n_sq[k], TB)
                rsqrt(D).then_inc(n_rs[k], 1)
                dve.wait_ge(n_rs[k], 1)
                for b in range(0, TB, 2):
                    v.tensor_scalar(tile[:, b], src[:, b], rs_y[:, b:b + 1], None, ALU.mult).then_inc(n_x[k], 1)
                for n in tiles:
                    split_lo(n, n)
                for c in range(DC):
                    dve.wait_ge(n_hi[k], c + 1)
                    v.scalar_tensor_tensor(xT_lo[:, c], bank[:, c], norm_g[:, k, c:c + 1],
                                           xT_hi[:, c].bitcast(F32), ALU.mult, ALU.subtract).then_inc(n_lo[k], 1)

            v.memset(zero_b[:], 0.0)
            norm(0, x_sb, x_sb, (0, 1))
            dve.wait_ge(consts_out, 16 * 6)
            own.after(v.tensor_tensor(lam_p[:, 0], lam4[:, 0], lam4[:, 1], ALU.mult))
            own.after(v.tensor_tensor(lam_p[:, 1], lam4[:, 2], lam4[:, 3], ALU.mult))
            for k in range(2):
                v.tensor_reduce(lam_s[:, k:k + 1], lam_p[:, k], AX.X, ALU.add).then_inc(lam_dot, 1)
            v.tensor_copy(ident_b[:], ident[:]).then_inc(mask_ready, 1)
            v.tensor_copy(mask_b[:], mask_t[:]).then_inc(mask_ready, 1)
            own.after(v.memset(cu[:, 0:KCONV - 1], 0.0))
            own.after(v.tensor_scalar(subln_g[:], subln_g[:], 1.0 - LAM_INIT, None, ALU.mult))
            dve.wait_ge(lam_exp, 1)
            own.after(v.tensor_tensor(neg_lam[:], lam_s[:, 1:2], lam_s[:, 0:1], ALU.subtract))
            own.after(v.tensor_scalar(neg_lam[:], neg_lam[:], -LAM_INIT, None, ALU.add))

            def rope(n, which, h):
                dve.wait_ge(bank_free, n + 3)
                dve.wait_ge(qk_ready, h * 2 + (which + 1))
                own.end(v.tensor_tensor(rope_a[:], qk_raw[:, which], cos_t[:], ALU.mult))
                own.after(v.tensor_tensor(rope_b[:], qk_rot[:, which], sin_t[:], ALU.mult))
                own.after(v.tensor_tensor(rope_a[:], rope_a[:], rope_b[:], ALU.add))
                own.after(v.tensor_copy(qk_hi[:, which], rope_a[:]))
                v.tensor_tensor(qk_lo[:, which], rope_a[:], qk_hi[:, which].bitcast(F32), ALU.subtract)\
                    .then_inc(qk_ready, 1)

            def t_out(V, hi, lo):
                dve.wait_ge(t_hi, V + 1)
                n = hi.shape[1]
                src = bank[:, 6, 0:n * P].rearrange("p (c n) -> p c n", c=n)
                v.tensor_tensor(lo, src, hi.bitcast(F32), ALU.subtract).then_inc(t_lo, 1)

            def row_max(U, u):
                s, nk = u % 2, (u + 1) * P
                dve.wait_ge(scores_done, U + 1)
                v.tensor_reduce(nbias[:, s], bank[:, 2 + 2 * s:4 + 2 * s, 0:nk], AX.X, ALU.max, negate=True)\
                    .then_inc(bias_ready, 1)

            def combine(U, u):
                s, nk = u % 2, (u + 1) * P
                at = P * (u * (u + 1) // 2)
                dve.wait_ge(exp_done, U + 3)
                own.after(v.reciprocal(rz[:, s], zsum[:, s]))
                own.after(v.tensor_scalar(p1s[:, 0:nk], prob[:, s, 1, 0:nk], rz[:, s, 1:2], neg_lam[:, 0:1],
                                          ALU.mult, ALU.mult))
                v.scalar_tensor_tensor(dif[:, at:at + nk], prob[:, s, 0, 0:nk], rz[:, s, 0:1], p1s[:, 0:nk],
                                       ALU.mult, ALU.add).then_inc(dif_ready, 1)

            def first_scores(n, U, V):
                split_lo(n + 2, 1)
                t_out(V, v_hi[:], v_lo[:])
                row_max(U, 0)
                row_max(U + 1, 1)
                combine(U, 0)
                combine(U + 1, 1)
                split_lo(n + 3, 0)
                dve.wait_ge(bank_free, n + 4)
                v.tensor_tensor(cu[:, 2:2 + T], c_sb[:], u_sb[:], ALU.mult).then_inc(cu_ready, 1)

            def l1_body(h, last):
                n = h * L1_BODY + L1_PRE
                U = h * 4
                V = h * 5
                row_max(U + 2, 2)
                row_max(U + 3, 3)
                dve.wait_ge(cu_ready, h + 1)
                own.after(v.tensor_copy(cw_h[:].unsqueeze(1), cw[:, bass.ds(h, 1)]))
                own.after(v.tensor_scalar(z_a[:], cu[:, 0:T], cw_h[:, 0:1], None, ALU.mult))
                own.after(v.scalar_tensor_tensor(z_b[:], cu[:, 1:1 + T], cw_h[:, 1:2], z_a[:], ALU.mult, ALU.add))
                own.after(v.scalar_tensor_tensor(z_a[:], cu[:, 2:2 + T], cw_h[:, 2:3], z_b[:], ALU.mult, ALU.add))
                combine(U + 2, 2)
                combine(U + 3, 3)
                split_lo(n + 2, 1)
                t_out(V + 1, difT_hi[:, 0:3], difT_lo[:, 0:3])
                dve.wait_ge(bank_free, n + 3)
                own.after(v.tensor_tensor(z_b[:], z_a[:], b_sb[:], ALU.mult))
                own.after(v.tensor_copy(bzT_hi[:, bass.ds(h, 1)], z_b[:].unsqueeze(1)))
                v.tensor_tensor(bzT_lo[:, bass.ds(h, 1)], z_b[:].unsqueeze(1),
                                bzT_hi[:, bass.ds(h, 1)].bitcast(F32), ALU.subtract).then_inc(bz_ready, 1)
                split_lo(n + 3, 0)
                t_out(V + 2, difT_hi[:, TB:TB + 3], difT_lo[:, TB:TB + 3])
                if not last:
                    rope(n + 1, 0, h + 1)
                split_lo(n + 4, 1)
                t_out(V + 3, difT_hi[:, 0:TB], difT_lo[:, 0:TB])
                if not last:
                    rope(n + 2, 1, h + 1)
                split_lo(n + 5, 0)
                dve.wait_ge(o_squares, h * 4 + 5)
                rsqrt(P).then_inc(o_scale, 1)
                if not last:
                    first_scores(n + 4, U + 4, V + 4)
                v_on = V + (4 if last else 5)
                dve.wait_ge(t_hi, v_on + 1)
                v.scalar_tensor_tensor(attnT_lo[:, bass.ds(h, 1)], bank[:, 6].unsqueeze(1), subln_g[:, 0:1],
                                       attnT_hi[:, bass.ds(h, 1)].bitcast(F32), ALU.mult, ALU.subtract)\
                    .then_inc(t_lo, 1)

            split_lo(2, 0)
            rope(0, 0, 0)
            split_lo(3, 1)
            rope(1, 1, 0)
            dve.wait_ge(const_in, 16 * 2)
            v.tensor_copy(iota_b[:], iota_f[:])
            dve.wait_ge(key_hi, 1)
            v.tensor_tensor(keysT_lo[:], keys_sb[:], keysT_hi[:].bitcast(F32), ALU.subtract).then_inc(key_lo, 1)
            split_lo(4, 0)
            first_scores(3, 0, 0)
            with own.repeat(H - 1, 33) as h:
                l1_body(h, False)
            l1_body(H - 1, True)

            def half_mixed(n):
                dve.wait_ge(bank_free, n + 3)
                v.tensor_tensor(m_a[:], sgc[:], yc_sb[:], ALU.mult).then_inc(half_mix, 1)

            def mix(i, n):
                dve.wait_ge(bank_free, n + 3)
                own.after(v.tensor_tensor(m_b[:], sga[:], ya_sb[:], ALU.mult))
                dve.wait_ge(half_mix, i + 1)
                own.after(v.tensor_tensor(m_c[:], m_a[:], m_b[:], ALU.add))
                own.after(v.tensor_copy(mixT_hi[:, bass.ds(i, 1)], m_c[:].unsqueeze(1)))
                v.tensor_tensor(mixT_lo[:, bass.ds(i, 1)], m_c[:].unsqueeze(1),
                                mixT_hi[:, bass.ds(i, 1)].bitcast(F32), ALU.subtract).then_inc(mix_done, 1)

            dve.wait_ge(t_lo, 5 * H + 1)
            half_mixed(N_L2 + 2)
            with own.repeat(DC - 1, 3) as i:
                n = i * 4 + (N_L2 + 3)
                split_lo(n + 2, 1)
                split_lo(n + 3, 0)
                mix(i, n + 1)
                split_lo(n + 4, 1)
                split_lo(n + 5, 0)
                half_mixed(n + 3)
            split_lo(N_WO + 1, 1)
            mix(DC - 1, N_WO - 1)
            for c in range(DC - 1):
                split_lo(N_WO + c + 2, c)
            dve.wait_ge(x_again, 16)
            for b in range(TB):
                if b < TB - 1:
                    dve.wait_ge(wo_done, b + 1)
                else:
                    dve.wait_ge(w_used, N_PQ + 2)
                for q in range(2):
                    half = h_sb[:, b, q * 512:(q + 1) * 512]
                    v.tensor_tensor(half, bank[:, 2 * b + q], half, ALU.add).then_inc(h_ready, 1)
            norm(1, h_sb, xn_2, (N_PQ + 1,))

            def q_out(s, c):
                dve.wait_ge(q_hi_done, s + 1)
                v.tensor_tensor(q_lo[:, c], bank[:, c], q_hi[:, c].bitcast(F32), ALU.subtract).then_inc(q_done, 1)

            q_out(0, 0)
            split_lo(N_PQ + 2, 0)
            with dve.Fori(0, PH - 1) as h:
                s = h * 2
                q_out(s + 1, 1)
                split_lo(s + (N_PQ + 3), 1)
                q_out(s + 2, 0)
                split_lo(s + (N_PQ + 4), 0)
            q_out(15, 1)
            split_lo(N_PQ + 17, 1)

            units = score[:].rearrange("p b h c n -> p (b h) c n")
            cand_flat = cand[:].rearrange("p a b -> p (a b)")
            val_out = sel[:, 2].rearrange("p b h k -> p (b h) k")
            key_out = sel[:, 0:2].rearrange("p c b h k -> p c (b h) k")

            def unit_step(i, j, halves, pairs, between=None):
                jobs = []
                if pairs:
                    jobs.append((cval, cidx, cand_flat, cand2[:]))
                if halves:
                    jobs += [(tval[:, c], tidx[:, c], sw[:, c], sw2[:, c]) for c in range(2)]
                if pairs:
                    v.tensor_copy(tidx_b[:], tidx[:])
                    v.tensor_tensor(cand[:], tval[:, 0].unsqueeze(2).to_broadcast([P, TOPK, TOPK]),
                                    tval[:, 1].unsqueeze(1).to_broadcast([P, TOPK, TOPK]), ALU.add)
                if halves:
                    v.tensor_copy(sw[:].unsqueeze(1), units[:, bass.ds(j, 1)])
                dve.drain()
                for val, idx, src, spare in jobs:
                    v.max(val[:, 0:8], src)
                dve.drain()
                for val, idx, src, spare in jobs:
                    v.match_replace(spare, val[:, 0:8], src, LOW)
                    v.max_index(idx[:, 0:8], val[:, 0:8], src)
                dve.drain()
                for val, idx, src, spare in jobs:
                    v.max(val[:, 8:16], spare)
                dve.drain()
                for val, idx, src, spare in jobs:
                    v.max_index(idx[:, 8:16], val[:, 8:16], spare)
                if between:
                    between()
                dve.drain()
                if not pairs:
                    return
                v.tensor_copy(val_out[:, bass.ds(i, 1)], cval[:].unsqueeze(1))
                own.end(v.tensor_single_scalar(crank[:, 0], cidx[:], 4, ALU.arith_shift_right))
                own.after(v.tensor_single_scalar(crank[:, 1], cidx[:], TOPK - 1, ALU.bitwise_and))
                own.after(v.tensor_copy(crank_b[:], crank[:].rearrange("p c k -> p (c k)").unsqueeze(2)
                                        .to_broadcast([P, 2 * TOPK, 2])))
                shape = [P, 2 * TOPK, TOPK // 2, 2]
                ranks = iota_b[:, 0:TOPK].rearrange("p (k j) -> p k j", j=2).unsqueeze(1).to_broadcast(shape)
                own.after(v.tensor_tensor(pick[:].rearrange("p r (k j) -> p r k j", j=2),
                                          crank_b[:].unsqueeze(2).to_broadcast(shape), ranks, ALU.is_equal))
                by_half = [t[:].rearrange("p (c r) k -> p c r k", c=2) for t in (pick, pick2)]
                own.after(v.tensor_tensor(by_half[1], by_half[0],
                                          tidx_b[:].unsqueeze(2).to_broadcast([P, 2, TOPK, TOPK]), ALU.mult))
                for c in range(2):
                    v.tensor_reduce(key_out[:, c, bass.ds(i, 1)], by_half[1][:, c].unsqueeze(1), AX.X, ALU.add)

            dve.wait_ge(s_copied, 2 * PH + 2)
            v.tensor_copy(sw[:].unsqueeze(1), units[:, 0:1])
            dve.drain()
            unit_step(0, 0, True, False)
            with own.repeat(31, 5) as i:
                c = i * 2
                unit_step(i, i + 1, True, True, lambda: split_lo(c + (N_A + 2), 0))
                split_lo(c + (N_A + 3), 1)
            unit_step(31, 0, False, True, lambda: split_lo(N_A + 64, 0))
            dve.drain().then_inc(keys_ready, 1)

            top = sel[:, 2].rearrange("p b h k -> p (b h) k")
            best = gsum[:].unsqueeze(2)
            own.after(v.tensor_copy(best, top[:, :, 0:1]))
            v.tensor_tensor(top, top, best.to_broadcast([P, PH * TB, TOPK]), ALU.subtract).then_inc(top_shift, 1)
            split_lo(N_A + 65, 1)
            dve.wait_ge(gate_exp, 1)
            own.after(v.tensor_reduce(gsum[:], top, AX.X, ALU.add))
            own.after(v.reciprocal(grec[:], gsum[:]))
            v.tensor_tensor(top, top, grec[:].unsqueeze(2).to_broadcast([P, PH * TB, TOPK]), ALU.mult)\
                .then_inc(sel_ready, 1)

            def bodies(t):
                return t.rearrange("p (b t) -> p b t", t=TOK)

            gateT = bank[:, 0]
            dve.wait_ge(selT_done, 3)
            own.after(v.tensor_copy(selT[:, :, 2], bodies(gateT)))
            own.after(v.tensor_tensor(bodies(grest[:]), bodies(gateT), selT[:, :, 2], ALU.subtract))
            own.after(v.tensor_copy(selT[:, :, 3], bodies(grest[:])))
            v.tensor_tensor(selT[:, :, 4], bodies(grest[:]), selT[:, :, 3], ALU.subtract).then_inc(sel_used, 1)
            dve.wait_ge(sel_used, 3)

            def spread_out(i, s):
                def keys4(t):
                    return t.rearrange("p t (k j) -> p t k j", j=4)

                def value(which):
                    row = which * TOK + s * 8
                    return tok5[:, row:row + 8].unsqueeze(2).to_broadcast([P, 8, NKEY // 4, 4])

                keys = iota_b[:].rearrange("p (k j) -> p k j", j=4).unsqueeze(1).to_broadcast([P, 8, NKEY // 4, 4])
                dve.wait_ge(g_full, i * 4 + (2 * s + 1))
                own.after(v.tensor_tensor(keys4(hit[:, s]), keys, value(0), ALU.is_equal))
                v.tensor_tensor(keys4(onehot[:, s, 0]), keys, value(1), ALU.is_equal)
                for q in range(3):
                    ins = v.tensor_tensor(keys4(onehot[:, s, 1 + q]), keys4(hit[:, s]), value(2 + q), ALU.mult)
                ins.then_inc(onehot_done[s], 1)

            def next_tok5(i):
                own.after(v.tensor_copy(tok5[:].unsqueeze(1),
                                        selT[:, bass.ds(i, 1)].rearrange("p o a t -> p o (a t)").unsqueeze(3)
                                        .to_broadcast([P, 1, 5 * TOK, 4])))

            next_tok5(0)
            spread_out(0, 0)
            split_lo(N_A + 66, 0)
            with own.repeat(31, 3) as i:
                spread_out(i, 1)
                split_lo(i * 2 + (N_A + 67), 1)
                for s in range(2):
                    dve.wait_ge(onehot_done[s], i + 1)
                next_tok5(i + 1)
                spread_out(i + 1, 0)
                split_lo(i * 2 + (N_A + 68), 0)
            spread_out(31, 1)
            dve.wait_ge(g_copied, T // 4 - 2)
            v.tensor_copy(g_buf[:, 0, BODIES - 2], g_stage[:, 0:8]).then_inc(g_last, 1)
            dve.wait_ge(g_copied, T // 4 + 2)
            v.tensor_copy(g_buf[:, 0, BODIES - 1], g_stage_end[:, 0:8]).then_inc(g_last, 1)

            def product(c, k, slot, e, landed):
                dve.wait_ge(gb_in[slot], landed)
                dve.wait_ge(hb_in[k], (c - k) * 8 + 16)
                dve.wait_ge(act_lo_done, c + 1)
                v.tensor_tensor(prod[:, k].rearrange("p (b t) -> p b t", t=TOK),
                                h_buf[:, k].rearrange("p (b t) -> p b t", t=TOK),
                                g_buf[:, slot, :, e].rearrange("p b e t -> p b (e t)"), ALU.mult)\
                    .then_inc(prod_done, 1)
                dve.wait_ge(act_hi_done, c + 1)
                v.tensor_tensor(act_lo[:, k], prod[:, k], act_hi[:, k].bitcast(F32), ALU.subtract)\
                    .then_inc(act_lo_done, 1)

            def b_eight(o, slot, last=False):
                def two(r, split):
                    for k in range(2):
                        c = o * 16 + r * 2 + (8 * slot + k)
                        product(c, k, slot, bass.ds(r * 2 + k, 1), o * 32 + 32)
                        if split:
                            split_lo(c + (N_B + 1), k + 1)

                with dve.Fori(0, 3 if last else 4) as r:
                    two(r, True)
                if last:
                    product(126, 0, slot, bass.ds(6, 1), 256)
                    split_lo(N_B + 127, 1)
                    product(127, 1, slot, bass.ds(7, 1), 256)

            dve.wait_ge(g_last, 2)
            with dve.Fori(0, 7) as o:
                b_eight(o, 0)
                b_eight(o, 1)
            b_eight(7, 0)
            b_eight(7, 1, last=True)

            for b in range(TB):
                dve.wait_ge(y_done, b + 1)
                for q in range(2):
                    half = h_sb[:, b, q * 512:(q + 1) * 512]
                    v.tensor_tensor(half, bank[:, 2 * b + q], half, ALU.add).then_inc(y_sum, 1)
            dve.wait_ge(y_sum, 2 * TB)
            own.end(v.tensor_tensor(o_sb[:, TB - 1], h_sb[:, TB - 1], gfin[:], ALU.mult))
            dve.wait_ge(y_sq, TB)
            rsqrt(D).then_inc(y_rs, 1)
            dve.wait_ge(y_rs, 1)
            for b in range(TB - 1):
                v.scalar_tensor_tensor(o_sb[:, b], h_sb[:, b], rs_y[:, b:b + 1], gfin[:], ALU.mult, ALU.mult)\
                    .then_inc(o_ready, 1)

        @block.tensor
        def _(pe):
            def three(dst, a_hi, a_lo, b_hi, b_lo, start, stop, **kw):
                pe.matmul(dst, a_hi, b_hi, start=start, stop=False, **kw)
                pe.matmul(dst, a_hi, b_lo, start=False, stop=False, **kw)
                return pe.matmul(dst, a_lo, b_hi, start=False, stop=stop, **kw)

            def norm(k, tile):
                pe.wait_ge(n_x[k], TB)
                for c in range(DC):
                    for b in range(TB):
                        last = pe.transpose(bank[:, c, b * P:(b + 1) * P], tile[:, b, c * P:(c + 1) * P], ident[:])
                    last.then_inc(n_t[k], 1)

            pe.wait_ge(ident_in, 16 * 2)
            norm(0, x_sb)

            def section(n, par, rhs_hi=xT_hi, rhs_lo=xT_lo, free=bank_free, freed=0, normed=None):
                s = par % 2
                pe.wait_ge(w_lo_done, n + 3)
                pe.wait_ge(free, n + (1 - freed))
                a_hi, a_lo = w_tile(w_hi, s), w_tile(w_lo, s)
                for c in range(DC):
                    if normed is not None:
                        pe.wait_ge(n_lo[normed], c + 1)
                    last = three(bank[:, s], a_hi[:, c], a_lo[:, c], rhs_hi[:, c], rhs_lo[:, c], c == 0, c == DC - 1)
                last.then_inc(w_used, 1)

            def scores(U, u):
                s, nk = u % 2, (u + 1) * P
                pe.wait_ge(exp_done, U + 1)
                for m in range(2):
                    rows = slice(m * HD, (m + 1) * HD)
                    scores_m = bank[:, 2 + 2 * s + m]
                    three(scores_m[:, 0:nk], qk_hi[rows, 0, u * P:nk], qk_lo[rows, 0, u * P:nk],
                          qk_hi[rows, 1, 0:nk], qk_lo[rows, 1, 0:nk], True, False)
                    last = pe.matmul(scores_m[:, u * P:nk], ident_b[:], mask_b[:], start=False, stop=True)
                last.then_inc(scores_done, 1)

            def t_wait(V):
                pe.wait_ge(t_lo, V + 1)

            def turn(U, V, units):
                pe.wait_ge(dif_ready, U + (units[-1] + 3))
                t_wait(V)
                first = P * (units[0] * (units[0] + 1) // 2)
                for c in range(sum(u + 1 for u in units)):
                    at = first + c * P
                    last = pe.transpose(bank[:, 6, c * P:(c + 1) * P], dif[:, at:at + P], ident[:])
                last.then_inc(t_full, 1)

            def attend(V, u, first):
                pe.wait_ge(t_lo, V + 2)
                for c in range(u + 1):
                    last = three(bank[:, 7, u * P:(u + 1) * P], difT_hi[:, first + c], difT_lo[:, first + c],
                                 v_hi[:, c], v_lo[:, c], c == 0, c == u)
                last.then_inc(pv_done, 1)

            def first_scores(n, U, V, h):
                section(n, 1)
                pe.wait_ge(bank_free, n + 2)
                t_wait(V)
                for b in range(TB):
                    ins = pe.transpose(bank[:, 6, b * P:(b + 1) * P], vT_sb[:, b * P:(b + 1) * P], ident[:])
                ins.then_inc(t_full, 1)
                pe.wait_ge(qk_ready, h * 2 + 3)
                scores(U, 0)
                scores(U + 1, 1)
                section(n + 1, 0)

            def l1_body(h, last):
                n = h * L1_BODY + L1_PRE
                U = h * 4
                V = h * 5
                scores(U + 2, 2)
                scores(U + 3, 3)
                section(n, 1)
                turn(U, V + 1, (0, 1))
                section(n + 1, 0)
                pe.wait_ge(on_ready, h + 1)
                attend(V + 1, 0, 0)
                attend(V + 1, 1, 1)
                turn(U, V + 2, (2,))
                section(n + 2, 1)
                attend(V + 2, 2, TB)
                turn(U, V + 3, (3,))
                if last:
                    pe.wait_ge(bz_ready, H + 1)
                    section(n + 3, 0, bzT_hi, bzT_lo)
                else:
                    section(n + 3, 0)
                attend(V + 3, 3, 0)
                if not last:
                    first_scores(n + 4, U + 4, V + 4, h + 1)
                else:
                    section(N_L2 + 3, 1)
                pe.wait_ge(on_ready, h + 2)
                t_wait(V + (4 if last else 5))
                for u in range(TB):
                    ins = pe.transpose(bank[:, 6, u * P:(u + 1) * P], on_sb[:, u], ident[:])
                ins.then_inc(t_full, 1)

            for n in range(3):
                section(n, n, normed=0 if n == 0 else None)
            pe.wait_ge(mask_ready, 2)
            first_scores(3, 0, 0, 0)
            with pe.Fori(0, H - 1) as h:
                l1_body(h, False)
            l1_body(H - 1, True)

            def ga_yc(n):
                section(n + 2, 1)
                section(n + 3, 0, bzT_hi, bzT_lo)

            pe.wait_ge(t_lo, 5 * H + 1)
            section(N_L2 + 4, 0, attnT_hi, attnT_lo)
            ga_yc(N_L2 + 3)
            with pe.Fori(0, DC - 2) as i:
                n = i * 4 + (N_L2 + 7)
                section(n, 1)
                section(n + 1, 0, attnT_hi, attnT_lo)
                ga_yc(n)
            section(N_WO - 1, 1, attnT_hi, attnT_lo)

            def add_rows(a_hi, a_lo, s, block_done=None, **kw):
                for b in range(TB):
                    if b and block_done is not None:
                        last.then_inc(block_done, 1)
                    for q in range(2):
                        cols = slice(q * 512, (q + 1) * 512)
                        last = three(bank[:, 2 * b + q], a_hi[:, b * P:(b + 1) * P], a_lo[:, b * P:(b + 1) * P],
                                     w_hi[:, s, cols], w_lo[:, s, cols], **kw)
                return last

            pe.wait_ge(bank_free, N_WO + 2)
            for c in range(DC):
                pe.wait_ge(mix_done, c + 2)
                pe.wait_ge(w_lo_done, N_WO + c + 3)
                last = c == DC - 1
                add_rows(mixT_hi[:, c], mixT_lo[:, c], c % 2, wo_done if last else None, start=c == 0, stop=last)\
                    .then_inc(w_used, 1)
            norm(1, xn_2)

            def key_scores(s, c):
                pe.wait_ge(q_done, s + 3)
                pe.wait_ge(key_lo, 1)
                pe.wait_ge(s_copied, s + 1)
                for b in range(TB):
                    toks = slice(b * P, (b + 1) * P)
                    last = three(bank[:, 2 + c, toks], q_hi[:, c, toks], q_lo[:, c, toks],
                                 keysT_hi[:, c], keysT_lo[:, c], True, True)
                last.then_inc(s_done, 1)

            def query(s, c, **kw):
                section(s + N_PQ, c, free=q_done, freed=N_PQ, **kw)

            query(0, 0, normed=1)
            with pe.Fori(0, PH - 1) as h:
                s = h * 2
                query(s + 1, 1)
                key_scores(s, 0)
                query(s + 2, 0)
                key_scores(s + 1, 1)
            query(15, 1)
            key_scores(14, 0)
            key_scores(15, 1)
            pe.wait_ge(s_copied, 2 * PH + 2)

            def experts(c, k):
                pe.wait_ge(w_lo_done, c + (N_A + 3))
                pe.wait_ge(gel_done, c + 1)
                u_hi, u_lo = w_tile(w_hi, k), w_tile(w_lo, k)
                for q in range(DC):
                    last = three(bank[:, 4 + k], u_hi[:, q], u_lo[:, q], xT_hi[:, q], xT_lo[:, q],
                                 q == 0, q == DC - 1)
                last.then_inc(w_used, 1)

            def spread(i, j):
                if j % 2 == 0:
                    pe.wait_ge(onehot_done[j // 2], i + 1)
                pe.wait_ge(g_copied, i * 4 + (j + 1))
                for t in range(4):
                    own_t = j % 2 * 4 + t
                    for q in range(3):
                        last = pe.matmul(bank[:, 6 + j % 2, t * P:(t + 1) * P], onehot[:, j // 2, 0, own_t],
                                         onehot[:, j // 2, 1 + q, own_t], start=q == 0, stop=q == 2)
                last.then_inc(g_full, 1)

            with pe.Fori(0, 32) as i:
                experts(i * 2, 0)
                experts(i * 2 + 1, 1)
            experts(64, 0)
            for q, at in enumerate((6, 7, 0)):
                pe.wait_ge(sel_ready if q == 2 else keys_ready, 1)
                for b in range(TB):
                    last = pe.transpose(bank[:, at, b * P:(b + 1) * P],
                                        sel[:, q, b].rearrange("p h k -> p (h k)"), ident[:])
                last.then_inc(selT_done, 1)
            with pe.Fori(0, 31) as i:
                experts(i * 2 + 65, 1)
                spread(i, 0)
                spread(i, 1)
                experts(i * 2 + 66, 0)
                spread(i, 2)
                spread(i, 3)
            experts(127, 1)
            for j in range(4):
                spread(31, j)

            pe.wait_ge(gel_done, NKEY + 2)
            for q in range(8):
                if q == 6:
                    pe.wait_ge(g_copied, T // 4 + 2)
                pe.matmul(bank[:, q], zero_b[:, 0:P], zero_b[:], start=True, stop=False)

            def b_chunk(c, k, **kw):
                pe.wait_ge(act_lo_done, c + 3)
                pe.wait_ge(w_lo_done, c + (N_B + 3))
                return add_rows(act_hi[:, k], act_lo[:, k], k, start=False, **kw)

            with pe.Fori(0, NKEY // 2 - 1) as i:
                for k in range(2):
                    b_chunk(i * 2 + k, k, stop=False).then_inc(w_used, 1)
            b_chunk(126, 0, stop=False).then_inc(w_used, 1)
            b_chunk(127, 1, block_done=y_done, stop=True).then_inc(y_done, 1)


def constants():
    import numpy as np
    f = np.float32
    inv = np.power(f(10000.0), -np.arange(0, HD, 2, dtype=f) / f(HD)).astype(f)
    ang = (np.arange(T, dtype=f)[None, :] * inv[:, None]).astype(f)
    cos, sin = np.cos(ang.astype(np.float64)).astype(f), np.sin(ang.astype(np.float64)).astype(f)
    row = np.arange(P)
    return {
        "c_cos": np.concatenate([cos] * 4),
        "c_sin": np.concatenate([-sin, sin] * 2),
        "c_ident": np.eye(P, dtype=f),
        "c_mask": np.where(row[None, :] <= row[:, None], f(0), f(-1e30)).astype(f),
        "c_iota": np.tile(row.astype(f), (P, 1)),
    }


def kernel(**inputs):
    import numpy as _np
    import concourse.bacc as _bacc
    from concourse import mybir as _mybir
    from concourse.bass_utils import run_bass_kernel_spmd as _run

    given = {name: _np.asarray(a) for name, a in inputs.items()}

    def tiles(w):
        return w.reshape(DC, P, -1, P).transpose(2, 1, 0, 3).reshape(-1, P, D)

    laid = {
        "x": given["x"],
        "norm_gains": _np.stack([given["norm1_g"][0], given["norm2_g"][0]]).reshape(2, DC, P).transpose(2, 0, 1),
        "w_in": tiles(given["w_in"][0]),
        "conv_w": given["conv_w"][0].reshape(KCONV, DC, P).transpose(2, 1, 0),
        "w_out_conv": tiles(given["w_out_conv"][0]),
        "lambdas": _np.stack([given[f"lambda_{n}"][0] for n in ("q1", "k1", "q2", "k2")]),
        "attn_subln_g": given["attn_subln_g"],
        "w_out_attn": tiles(given["w_out_attn"][0]),
        "w_o": given["w_o"],
        "peer_w_q": tiles(given["peer_w_q"][0]),
        "peer_keys": _np.stack([given["peer_keys1"][0].T, given["peer_keys2"][0].T], axis=1),
        "peer_u": tiles(given["peer_u"][0].T),
        "peer_v": given["peer_v"],
        "final_norm_g": given["final_norm_g"],
    }
    laid.update(constants())

    nc = _bacc.Bacc("TRN2", target_bir_lowering=False, num_devices=1)
    arrays, args = {}, []
    for name, value in laid.items():
        a = _np.ascontiguousarray(value)
        arrays[f"in_{name}"] = a
        args.append(nc.dram_tensor(f"in_{name}", a.shape, _mybir.dt.from_np(a.dtype), kind="ExternalInput").ap())
    args.append(nc.dram_tensor("out_0", (1, T, D), _mybir.dt.float32, kind="ExternalOutput").ap())
    peer_block(nc, *args)
    r = _run(nc, [arrays], core_ids=[0])
    return r.results[0]["out_0"]
```
